# Optimizing a Trainium2 kernel written in Bass

```python
import jax, jax.numpy as jnp
from jax import lax
import numpy as np

D_MODEL = 1024
BATCH = 1
SEQ = 512
DEPTH = 1

HGRN_HEADS = 8
HGRN_DK = 128
HGRN_DV = 128
HGRN_WIDTH = HGRN_HEADS * HGRN_DK
HGRN_CHUNK = 64
CONV_CH = D_MODEL // 2
CONV_WIDTH = 31
N_EXPERTS = 16
N_GROUPS = 4
EXPERTS_PER_GROUP = N_EXPERTS // N_GROUPS
TOP_K = 2
EXPERT_FF = 512
IN_COLS = 4 * HGRN_WIDTH + 2 * CONV_CH + 2 * D_MODEL
EPS = 1e-6

kernel_name = "hgrn2_conformer_gated_moe_adaln"

def _rmsnorm(x, g):
    xf = x.astype(jnp.float32)
    y = xf * lax.rsqrt(jnp.mean(xf * xf, axis=-1, keepdims=True) + EPS)
    return (y * g.astype(jnp.float32)).astype(x.dtype)

def _layernorm(x, g, b):
    xf = x.astype(jnp.float32)
    mu = jnp.mean(xf, axis=-1, keepdims=True)
    var = jnp.mean(jnp.square(xf - mu), axis=-1, keepdims=True)
    y = (xf - mu) * lax.rsqrt(var + EPS)
    return (y * g.astype(jnp.float32) + b.astype(jnp.float32)).astype(x.dtype)

def _modulate(h, shift, scale):
    return h * (1.0 + scale[:, None, :]) + shift[:, None, :]

def _hgrn2_chunkwise(q, k, v, log_f):
    B, S, H, DK = q.shape
    DV = v.shape[-1]
    N, C = S // HGRN_CHUNK, HGRN_CHUNK

    def to_chunks(t):
        return t.astype(jnp.float32).reshape(B, N, C, H, t.shape[-1]).transpose(1, 0, 3, 2, 4)

    qc, kc, vc = to_chunks(q), to_chunks(k), to_chunks(v)
    bc = jnp.cumsum(to_chunks(log_f), axis=-2)
    causal = jnp.tril(jnp.ones((C, C), dtype=bool))[:, :, None]

    def step(state, inp):
        q_, k_, v_, b_ = inp
        diff = b_[:, :, :, None, :] - b_[:, :, None, :, :]
        decay = jnp.where(causal, jnp.exp(jnp.where(causal, diff, 0.0)), 0.0)
        scores = jnp.einsum('bhtk,bhsk,bhtsk->bhts', q_, k_, decay)
        o_intra = jnp.einsum('bhts,bhsv->bhtv', scores, v_)
        o_inter = jnp.einsum('bhtk,bhkv->bhtv', q_ * jnp.exp(b_), state)
        b_last = b_[:, :, -1, :]
        k_dec = k_ * jnp.exp(b_last[:, :, None, :] - b_)
        new_state = jnp.exp(b_last)[..., None] * state + jnp.einsum('bhsk,bhsv->bhkv', k_dec, v_)
        return new_state, o_intra + o_inter

    state0 = jnp.zeros((B, H, DK, DV), jnp.float32)
    _, out = lax.scan(step, state0, (qc, kc, vc, bc))
    return out.transpose(1, 0, 3, 2, 4).reshape(B, S, H, DV).astype(v.dtype)

def _token_mixer(h, w_in, lb, onorm_g, w_o_hgrn, conv_w, conv_b, ln_g, ln_b, w_o_conv, w_out):
    B, S, _ = h.shape
    proj = h @ w_in
    cuts = [HGRN_WIDTH, 2 * HGRN_WIDTH, 3 * HGRN_WIDTH, 4 * HGRN_WIDTH,
            4 * HGRN_WIDTH + CONV_CH, 4 * HGRN_WIDTH + 2 * CONV_CH,
            4 * HGRN_WIDTH + 2 * CONV_CH + D_MODEL]
    q, fz, i, og, ca, cb, gate_a, gate_b = jnp.split(proj, cuts, axis=-1)

    f = lb + (1.0 - lb) * jax.nn.sigmoid(fz.astype(jnp.float32))
    log_f = jnp.log(f)
    k = (1.0 - f).astype(h.dtype)
    hs = (B, S, HGRN_HEADS, HGRN_DK)
    o = _hgrn2_chunkwise((q * (HGRN_DK ** -0.5)).reshape(hs), k.reshape(hs),
                         jax.nn.silu(i).reshape(B, S, HGRN_HEADS, HGRN_DV), log_f.reshape(hs))
    o = _rmsnorm(o, onorm_g).reshape(B, S, HGRN_HEADS * HGRN_DV) * jax.nn.silu(og)
    y_a = o @ w_o_hgrn

    u = ca * jax.nn.sigmoid(cb)
    kern = conv_w.astype(u.dtype).reshape(CONV_WIDTH, 1, CONV_CH)
    u = lax.conv_general_dilated(u, kern, window_strides=(1,), padding=[(CONV_WIDTH - 1, 0)],
                                 dimension_numbers=('NWC', 'WIO', 'NWC'),
                                 feature_group_count=CONV_CH) + conv_b
    u = jax.nn.silu(_layernorm(u, ln_g, ln_b))
    y_b = u @ w_o_conv

    merged = jax.nn.sigmoid(gate_a) * y_a + jax.nn.sigmoid(gate_b) * y_b
    return merged @ w_out

def _moe(h, w_router, router_bias, w_gate, w_up, w_down):
    B, S, D = h.shape
    T = B * S
    hf = h.reshape(T, D)
    scores = jax.nn.sigmoid((hf @ w_router).astype(jnp.float32))
    sel = scores + router_bias.astype(jnp.float32)
    grp = sel.reshape(T, N_GROUPS, EXPERTS_PER_GROUP)
    group_score = lax.top_k(grp, 2)[0].sum(-1)
    g_idx = jnp.argmax(group_score, axis=-1)
    in_grp = jnp.take_along_axis(grp, g_idx[:, None, None], axis=1)[:, 0]
    _, loc = lax.top_k(in_grp, TOP_K)
    e_idx = g_idx[:, None] * EXPERTS_PER_GROUP + loc
    w = jnp.take_along_axis(scores, e_idx, axis=1)
    w = w / jnp.sum(w, axis=-1, keepdims=True)
    comb = jnp.einsum('tk,tke->te', w, jax.nn.one_hot(e_idx, N_EXPERTS, dtype=jnp.float32)).astype(h.dtype)
    y = jnp.zeros_like(hf)
    for e in range(N_EXPERTS):
        a = jax.nn.silu(hf @ w_gate[e]) * (hf @ w_up[e])
        y = y + comb[:, e:e + 1] * (a @ w_down[e])
    return y.reshape(B, S, D)

def setup_inputs(seed: int = 0) -> dict:
    key = jax.random.key(seed)
    ks = jax.random.split(key, 24)
    f32 = jnp.float32

    def nrm(k, shape, scale):
        return jax.random.normal(k, shape, f32) * scale

    H_DV = HGRN_HEADS * HGRN_DV
    return {
        "x": nrm(ks[0], (BATCH, SEQ, D_MODEL), 1.0),
        "c": nrm(ks[1], (BATCH, D_MODEL), 1.0),
        "w_ada": nrm(ks[2], (DEPTH, D_MODEL, 6 * D_MODEL), 0.5 * D_MODEL ** -0.5),
        "b_ada": nrm(ks[3], (DEPTH, 6 * D_MODEL), 0.02),
        "norm_mix_g": 1.0 + nrm(ks[4], (DEPTH, D_MODEL), 0.02),
        "w_in": nrm(ks[5], (DEPTH, D_MODEL, IN_COLS), D_MODEL ** -0.5),
        "hgrn_lb_logits": nrm(ks[6], (DEPTH, HGRN_WIDTH), 0.5),
        "hgrn_onorm_g": 1.0 + nrm(ks[7], (DEPTH, HGRN_HEADS, HGRN_DV), 0.02),
        "w_o_hgrn": nrm(ks[8], (DEPTH, H_DV, D_MODEL), H_DV ** -0.5),
        "conv_w": nrm(ks[9], (DEPTH, CONV_WIDTH, CONV_CH), CONV_WIDTH ** -0.5),
        "conv_b": nrm(ks[10], (DEPTH, CONV_CH), 0.02),
        "conv_ln_g": 1.0 + nrm(ks[11], (DEPTH, CONV_CH), 0.02),
        "conv_ln_b": nrm(ks[12], (DEPTH, CONV_CH), 0.02),
        "w_o_conv": nrm(ks[13], (DEPTH, CONV_CH, D_MODEL), CONV_CH ** -0.5),
        "w_out": nrm(ks[14], (DEPTH, D_MODEL, D_MODEL), D_MODEL ** -0.5),
        "norm_ffn_g": 1.0 + nrm(ks[15], (DEPTH, D_MODEL), 0.02),
        "w_router": nrm(ks[16], (D_MODEL, N_EXPERTS), D_MODEL ** -0.5),
        "router_bias": nrm(ks[17], (N_EXPERTS,), 0.01),
        "w_gate_e": nrm(ks[18], (DEPTH, N_EXPERTS, D_MODEL, EXPERT_FF), D_MODEL ** -0.5),
        "w_up_e": nrm(ks[19], (DEPTH, N_EXPERTS, D_MODEL, EXPERT_FF), D_MODEL ** -0.5),
        "w_down_e": nrm(ks[20], (DEPTH, N_EXPERTS, EXPERT_FF, D_MODEL), EXPERT_FF ** -0.5),
        "final_norm_g": 1.0 + nrm(ks[21], (D_MODEL,), 0.02),
    }

def reference(x, c, w_ada, b_ada, norm_mix_g, w_in, hgrn_lb_logits, hgrn_onorm_g, w_o_hgrn,
              conv_w, conv_b, conv_ln_g, conv_ln_b, w_o_conv, w_out, norm_ffn_g,
              w_router, router_bias, w_gate_e, w_up_e, w_down_e, final_norm_g):
    p = jax.nn.softmax(hgrn_lb_logits.astype(jnp.float32), axis=0)
    lower_bounds = jnp.cumsum(p, axis=0) - p[0:1]
    c_act = jax.nn.silu(c)
    for l in range(DEPTH):
        mod = c_act @ w_ada[l] + b_ada[l]
        sh1, sc1, g1, sh2, sc2, g2 = jnp.split(mod, 6, axis=-1)
        h = _modulate(_rmsnorm(x, norm_mix_g[l]), sh1, sc1)
        x = x + g1[:, None, :] * _token_mixer(h, w_in[l], lower_bounds[l], hgrn_onorm_g[l], w_o_hgrn[l],
                                              conv_w[l], conv_b[l], conv_ln_g[l], conv_ln_b[l],
                                              w_o_conv[l], w_out[l])
        h = _modulate(_rmsnorm(x, norm_ffn_g[l]), sh2, sc2)
        x = x + g2[:, None, :] * _moe(h, w_router, router_bias, w_gate_e[l], w_up_e[l], w_down_e[l])
    return _rmsnorm(x, final_norm_g)


_drawn_inputs = setup_inputs


def setup_inputs(seed=0):
    import zlib

    import numpy as np

    out = dict(_drawn_inputs(seed))
    spreads = {}
    factors = {'norm_mix_g': 4.899,
     'hgrn_onorm_g': 22.958,
     'conv_b': 34.136,
     'conv_ln_g': 51.424,
     'conv_ln_b': 64.0,
     'final_norm_g': 7.608,
     'norm_ffn_g': 8.0,
     'router_bias': 8.0}
    for name, (base, spread) in spreads.items():
        noise = np.random.default_rng([zlib.crc32(name.encode()), seed]).standard_normal(out[name].shape)
        drawn = base * np.exp(spread * noise) if base else spread * noise
        out[name] = __import__('jax').numpy.asarray(drawn.astype(out[name].dtype))
    for name, factor in factors.items():
        out[name] = (out[name] * factor).astype(out[name].dtype)
    return out
```

```python
from contextlib import ExitStack

import concourse.bass as bass
from concourse import mybir
import numpy as np

F32 = mybir.dt.float32
F32R = mybir.dt.float32r
I32 = mybir.dt.int32
ACT = mybir.ActivationFunctionType
ALU = mybir.AluOpType
AX = mybir.AxisListType

P = 128
T = 512
D = 1024
KT = D // P
TT = T // P
QH = 4
DK = 128
QSCALE = DK ** -0.5
CC = 512
CT = CC // P
CW = 31
PADW = CW - 1
NE = 16
FF = 512
EPS = 1e-6
CHW = 256
NUNIT = QH * TT
NLEV = 7
NJ = 24
NPAIR = 2 * T
PADIDX = 1 << 14

C_C, C_BADA, C_GMIX, C_LB, C_ON = 0, 8, 24, 32, 40
C_CW, C_CB, C_LG, C_LB2, C_WR = 48, 48 + CT * CW, 52 + CT * CW, 56 + CT * CW, 60 + CT * CW
C_ALL = C_WR + KT * NE
K_ID, K_ONE, K_MD, K_MC, K_MV, K_TRI, K_JI = 0, 128, 256, 384, 512, 640, 768
K_ALL = 768 + NJ


def plan():
    chunks = [("cb", i) for i in range(2)] + [("ca", i) for i in range(2)]
    for qd in range(2):
        chunks += [(k, 2 * qd + i) for k in ("fz", "q", "iv", "og") for i in range(2)]
    chunks += [("gb", i) for i in range(4)] + [("yb", i) for i in range(2)]
    for i in range(4):
        chunks += [("ga", i), ("ya", i)]
    chunks += [("wo", i) for i in range(4)]
    steps = []
    for n, (kind, i) in enumerate(chunks):
        for t in range(4 if kind == "yb" else 2):
            steps.append((kind, (4 if kind == "yb" else 2) * i + t, n, t))
    return chunks, steps


def trunk_kernel(nc, xT, x, cols, consts, masks, vals, w_ada, b_ada_row, w_in, w_o_hgrn, w_o_conv,
                 w_out, router_bias, g_ffn, g_final, w_gate, w_up, w_down, h2_dram, y_dram,
                 idx_dram, out):
    chunks, steps = plan()
    at_step = {}
    for s, (kind, tile, _, _) in enumerate(steps):
        at_step[(kind, tile)] = s
    tmp_no = {}
    for s, (kind, tile, _, _) in enumerate(steps):
        if kind in ("iv", "og", "ga"):
            tmp_no[s] = len(tmp_no)

    sigs = [s for s, (kind, _, _, _) in enumerate(steps) if kind in ("iv", "og")]
    tmp_no2 = {s: n for n, s in enumerate(sigs)}

    ctx = ExitStack()
    with ctx:
        base = (nc.sbuf_base + 63) // 64 * 64
        top = [base]
        placed = {}

        def region(name, nbytes):
            placed[name] = top[0]
            top[0] += (nbytes + 63) // 64 * 64
            assert top[0] <= nc.sbuf_usable_end, (name, top[0])

        def at(name, where, shape, dt=F32, plus=0):
            return nc.alloc_sbuf_tensor_at(name, shape, dt, offset=placed[where] + plus)

        for r, n in (("HT", 32768), ("WRAW", 16384), ("WS", 32768), ("F", 8192), ("K", 8192),
                     ("Q", 8192), ("V", 8192), ("TOT", 8192), ("OG", 8192), ("DG", 8192),
                     ("ST", 8192), ("UACC", 4 * CT * (T + PADW) + 8192), ("CS", 16384),
                     ("ON0", 16384), ("COLS", 4 * C_ALL), ("CONST", 4 * K_ALL),
                     ("MASK", 4 * NLEV * 64), ("TMP", 4096), ("RST", 2048), ("SMALL", 1024)):
            region(r, n)

        h_hi = at("h_hi", "HT", [P, KT, T], F32R)
        h_lo = at("h_lo", "HT", [P, KT, T], F32R, 16384)
        w_raw = at("w_raw", "WRAW", [P, 2, 2048])
        w_hi = at("w_hi", "WS", [P, 2, 2048], F32R)
        w_lo = at("w_lo", "WS", [P, 2, 2048], F32R, 16384)
        f_t = at("f_t", "F", [P, QH, T])
        k_t = at("k_t", "K", [P, QH, T])
        q_t = at("q_t", "Q", [P, QH, T])
        v_t = at("v_t", "V", [P, TT, QH * DK])
        og_t = at("og_t", "OG", [P, QH, T])
        dg_t = at("dg_t", "DG", [P, QH, T])
        st_t = at("st_t", "ST", [P, NUNIT, P])
        o_t = at("o_t", "ST", [P, QH, T])
        kd_t = at("kd_t", "TOT", [P, 3 * QH, P])
        ss_t = at("ss_t", "DG", [P, 3, QH * DK])
        tot = [f_t]
        off = {1: 0, 2: 4096, 3: 6144, 4: 7168, 5: 7680, 6: 7936, 7: 8064}
        for l in range(1, NLEV + 1):
            tot.append(at(f"tot{l}", "TOT", [P, 2048 >> l], F32, off[l]))
        u_t = at("u_t", "UACC", [P, CT, T + PADW])
        usq = at("usq", "UACC", [P, CT, T])
        acc = at("acc", "UACC", [P, CT, T], F32, 4 * CT * (T + PADW))
        cs_hi = at("cs_hi", "CS", [P, CT, T], F32R)
        cs_lo = at("cs_lo", "CS", [P, CT, T], F32R, 8192)
        xt_t = at("xt_t", "ON0", [P, KT, T])
        xsq = at("xsq", "CS", [P, KT, T])
        ada_w = [at(f"ada_w{i}", r, [P, KT, CHW]) for i, r in
                 enumerate(("F", "K", "Q", "V", "TOT", "OG", "DG", "ST"))]
        on_hi = [at("on0_hi", "ON0", [P, QH, T], F32R), at("on1_hi", "Q", [P, QH, T], F32R)]
        on_lo = [at("on0_lo", "ON0", [P, QH, T], F32R, 8192), at("on1_lo", "V", [P, QH, T], F32R)]
        mb_t = [at("mb0", "F", [P, 4, T]), at("mb1", "K", [P, 4, T])]
        m_hi = at("m_hi", "UACC", [P, KT, T], F32R)
        m_lo = at("m_lo", "TOT", [P, KT, T], F32R)
        ada_acc = at("ada_acc", "CS", [P, 4, D])
        ada_p = [at("ada_p0", "DG", [P, KT, CHW]), at("ada_p1", "ST", [P, KT, CHW])]
        rows = at("rows", "ON0", [P, 4, D])
        x2_t = at("x2_t", "Q", [P, TT, D])
        h2_t = at("h2_t", "F", [P, TT, D])
        h2T = at("h2T", "TOT", [P, KT, T])
        gffn = at("gffn", "TMP", [P, D])
        cols_t = at("cols_t", "COLS", [P, C_ALL])
        con_t = at("con_t", "CONST", [P, K_ALL])
        mask_t = at("mask_t", "MASK", [P, NLEV * 64], I32)
        tmp = at("tmp", "TMP", [P, 2, T])
        rst = at("rst", "RST", [P, T])
        mod1 = at("mod1", "SMALL", [P, 16])
        cact = at("cact", "SMALL", [P, 8], F32, 64)
        lbc = at("lbc", "SMALL", [P, 32], F32, 96)
        eps_c = at("eps_c", "SMALL", [P, 1], F32, 224)
        nst = at("nst", "SMALL", [P, 8], F32, 256)
        wsel = at("wsel", "SMALL", [P, 2, TT], F32, 288)
        jobs_i = at("jobs_i", "SMALL", [P, NJ + 8], I32, 320)
        vals_t = at("vals_t", "SMALL", [P, 2 * TT], I32, 448)
        pos_i = at("pos_i", "SMALL", [P, 2 * TT], I32, 480)
        idx_s = at("idx_s", "SMALL", [P, NJ], I32, 512)
        idx_g = at("idx_g", "SMALL", [P, NJ], I32, 608)
        gi = at("gi", "SMALL", [P, 1], I32, 704)
        si = at("si", "SMALL", [P, 1], I32, 736)
        rb_t = at("rb_t", "SMALL", [P, NE], F32, 768)
        spacer = [at(f"spacer{i}", "SMALL", [P, 1], F32, 832 + 32 * i) for i in range(2)]
        e_raw = [at(f"e_raw{c}", r, [P, 2048], F32, o) for c, (r, o) in
                 enumerate((("WRAW", 0), ("WRAW", 8192), ("DG", 0), ("ON0", 0), ("OG", 0), ("ST", 0)))]
        slot_at = (("HT", 0), ("HT", 16384), ("WS", 0), ("WS", 16384), ("UACC", 0), ("CS", 0))
        e_hi = [at(f"e_hi{c}", r, [P, 2048], F32R, o) for c, (r, o) in enumerate(slot_at)]
        e_lo = [at(f"e_lo{c}", r, [P, 2048], F32R, o + 8192) for c, (r, o) in enumerate(slot_at)]
        xg = at("xg", "F", [P, D])
        y_sb = at("y_sb", "F", [P, D], F32, 4096)
        he_hi = at("he_hi", "F", [P, KT * P], F32R, 8192)
        he_lo = at("he_lo", "F", [P, KT * P], F32R, 12288)
        sg_t = at("sg_t", "TOT", [P, FF])
        a_t = at("a_t", "TOT", [P, FF], F32, 2048)
        ae_hi = at("ae_hi", "TOT", [P, 4 * P], F32R, 4096)
        ae_lo = at("ae_lo", "TOT", [P, 4 * P], F32R, 6144)
        gfin = at("gfin", "TMP", [P, D])
        fin = [at("fin0", "HT", [P, 2, D]), at("fin1", "HT", [P, 2, D], F32, 8192),
               at("fin2", "HT", [P, 2, D], F32, 16384), at("fin3", "HT", [P, 2, D], F32, 24576)]
        fsq = at("fsq", "ST", [P, D])
        rt = at("rt", "ST", [P, 32, TT * NE])

        proj = ctx.enter_context(nc.psum_tensor("proj", [P, 2, 512], F32))
        pp = ctx.enter_context(nc.psum_tensor("pp", [P, 1024], F32))
        ha = ctx.enter_context(nc.psum_tensor("ha", [P, 4, 512], F32))

        ident = con_t[:, K_ID:K_ID + P]
        ones = con_t[:, K_ONE:K_ONE + P]
        mean_d = con_t[:, K_MD:K_MD + P]
        mean_c = con_t[:, K_MC:K_MC + P]
        mean_v = con_t[:, K_MV:K_MV + P]
        tri = con_t[:, K_TRI:K_TRI + P]

        sem = lambda name: ctx.enter_context(nc.semaphore(name))
        s_par = sem("params_loaded")
        s_xt = sem("xT_loaded")
        s_ada = [sem(f"ada_piece{i}_loaded") for i in range(8)]
        s_raw = [sem(f"raw_chunk_loaded{i}") for i in range(2)]
        s_hi = sem("chunk_hi_done")
        s_lo = sem("chunk_lo_done")
        s_tile = sem("tile_done")
        s_free = [sem(f"tile_evacuated{i}") for i in range(2)]
        s_sig = sem("sigmoid_in_tmp")
        s_xsq = sem("xsq_done")
        s_p0 = sem("pre_pe")
        s_eps = sem("eps_set")
        s_cs = sem("c_sigmoid_done")
        s_ca = sem("c_silu_done")
        s_sq0 = sem("x_root_done")
        s_rdone0 = sem("x_root_inverted")
        s_rdone = sem("x_normed")
        s_md = sem("ada_columns_done")
        s_lb = sem("lower_bounds_done")
        s_h32 = sem("h_float32")
        s_hh = sem("h_hi_done")
        s_hl = sem("h_lo_done")
        s_pad = sem("conv_pad_zeroed")
        s_fd = sem("forget_done")
        s_k = sem("k_done")
        s_dg = sem("dg_done")
        s_lvl = sem("level_done")
        s_st = sem("scores_set")
        s_qu = sem("q_updated")
        s_ku = sem("k_updated")
        s_tot = sem("totals_done")
        s_x1 = sem("kdec_transposed")
        s_kd = sem("kdec_copied")
        s_x2 = sem("state_updates_done")
        s_ss = sem("states_done")
        s_x3 = sem("o_done")
        s_oc = sem("o_copied")
        s_x4 = sem("o_meansq_done")
        s_rt = sem("o_root_done")
        s_or = sem("o_normed")
        s_oo = sem("o_gated")
        s_oh = sem("on_hi_done")
        s_ol = sem("on_lo_done")
        s_cv = sem("conv_steps")
        s_cz = sem("conv_silu_done")
        s_l1 = sem("ln_pe")
        s_ld = sem("ln_dve")
        s_la = sem("ln_act")
        s_ch = sem("cs_hi_done")
        s_cl = sem("cs_lo_done")
        s_mp = sem("merged_sum")
        s_mh = sem("merged_hi_done")
        s_ml = sem("merged_lo_done")
        s_az = sem("ada_acc_zeroed")
        s_ab = sem("ada_bias_loaded")
        s_ap = [sem(f"ada_rest_loaded{i}") for i in range(2)]
        s_aa = sem("ada_accumulated")
        s_ar = sem("ada_rows_pe")
        s_rw = sem("ada_rows_copied")
        s_x = sem("x_loaded")
        s_gf = sem("gffn_loaded")
        s_x2d = sem("x2_done")
        s_xs = sem("x2_act")
        s_n2 = sem("norm2_dve")
        s_h2 = sem("h2_done")
        s_h2w = sem("h2_written")
        s_h2p = sem("h2_transposed")
        s_h2c = sem("h2T_copied")
        s_lg = sem("logits_done")
        s_sc = sem("router_scores")
        s_r = sem("routing_steps")
        s_ps = sem("positions_done")
        s_dv = sem("choices_done")
        s_rk = sem("ranks_done")
        s_pf = sem("index_table_filled")
        s_ix = sem("indices_scattered")
        s_il = sem("indices_loaded")
        s_ig = sem("gather_indices_done")
        s_jb = sem("job_table_done")
        s_er = [sem(f"expert_raw{c}_loaded") for c in range(6)]
        s_hg = sem("gate_up_hi_done")
        s_lg2 = sem("gate_up_lo_done")
        s_hd = sem("down_hi_done")
        s_ld2 = sem("down_lo_done")
        s_eu = [sem(f"expert_slot_used{c}") for c in range(6)]
        s_gc = sem("gather_index_copied")
        s_g = sem("tokens_gathered")
        s_xp = sem("tokens_transposed")
        s_heh = sem("tokens_hi_done")
        s_hel = sem("tokens_lo_done")
        s_gt = sem("gate_done")
        s_up = sem("up_done")
        s_sg = sem("silu_done")
        s_a = sem("act_done")
        s_ad = sem("act_transposed")
        s_aeh = sem("act_hi_done")
        s_ael = sem("act_lo_done")
        s_y = sem("y_evacuated")
        s_yc = sem("scatter_index_copied")
        s_sp = [sem(f"spacer{i}_set") for i in range(2)]
        s_ys = sem("pool_stores")
        s_fl = [sem(f"final_loaded{i}") for i in range(TT)]
        s_gl = sem("final_gain_loaded")
        s_f1 = sem("final_first_added")
        s_f2 = sem("final_second_added")
        s_fr = sem("final_root_inverted")
        s_fo = sem("final_done")
        s_fa = sem("final_act")
        s_out = sem("out_written")

        block = ctx.enter_context(nc.Block())

        def evacuated(eng, s):
            eng.wait_ge(s_free[s % 2], s // 2 + 1)

        def tile_ready(eng, s):
            eng.wait_ge(s_tile, s + 1)

        last_step = {n: s for s, (_, _, n, _) in enumerate(steps)}

        def chunk_used(eng, n):
            eng.wait_ge(s_tile, last_step[n] + 1)

        def tblk(ap, m, half):
            return ap.rearrange("p (b two m) -> p b two m", two=2, m=m)[:, :, half, :]

        def flat(t):
            return t[:, :, :].rearrange("p h t -> p (h t)") if len(t.shape) == 3 else t[:, :]

        SLOT = {}

        def place(step, what):
            SLOT.setdefault(step, []).append(what)

        for qd in range(2):
            s0 = at_step[("q", 4 * qd + 3)] + 1
            for l in range(NLEV + 1):
                place(s0 + l, ("lev", qd, l))
            for n, x_ in enumerate(("x1", "x2", "x3", "x4")):
                place(s0 + NLEV + 1 + n, (x_, qd))
        place(40, ("ln", 0))
        place(42, ("ln", 1))
        row_step = at_step[("ya", 7)]
        place(row_step, ("row", 0))
        place(row_step + 2, ("row", 1))

        def chunk_source(n):
            kind, i = chunks[n]
            win = w_in[0].rearrange("(k p) n -> p k n", p=P)
            o = {"q": 0, "fz": 1024, "iv": 2048, "og": 3072, "ca": 4096, "cb": 4608,
                 "ga": 5120, "gb": 6144}
            if kind in o:
                return win[:, :, o[kind] + CHW * i:o[kind] + CHW * (i + 1)]
            if kind == "yb":
                return w_o_conv[0].rearrange("(k p) n -> p k n", p=P)[:, :, 512 * i:512 * (i + 1)]
            w = w_o_hgrn if kind == "ya" else w_out
            return w[0].rearrange("(k p) n -> p k n", p=P)[:, :, CHW * i:CHW * (i + 1)]

        def chunk_view(ap, n):
            return ap[:, n % 2, :].rearrange("p (k n) -> p k n", k=4 if chunks[n][0] == "yb" else 8)

        def expert_view(ap, c):
            return ap[:, :].rearrange("p (k n) -> p k n", k=2 if c >= 4 else 4)

        def expert_load(eng, e, c):
            w, kk = (w_gate, 4) if c < 2 else (w_up, 4) if c < 4 else (w_down, 2)
            src = w[0].rearrange("e (k p) n -> p e k n", p=P)[:, bass.ds(e, 1), kk * (c % 2):kk * (c % 2) + kk, :]
            eng.dma_start(e_raw[c][:, :].rearrange("p (o k n) -> p o k n", o=1, k=kk), src).then_inc(s_er[c], 16)

        NCH = len(chunks)

        gn = chunks.index(("ga", 0))

        @block.sync
        def _(sp):
            sp.dma_start(cols_t[:, :], cols).then_inc(s_par, 16)
            sp.dma_start(con_t[:, :], consts).then_inc(s_par, 16)
            sp.dma_start(mask_t[:, :], masks).then_inc(s_par, 16)
            sp.dma_start(vals_t[:, :], vals).then_inc(s_par, 16)
            sp.dma_start(rb_t[:, :], router_bias.broadcast_to([P, NE])).then_inc(s_par, 16)
            sp.dma_start(xt_t[:, :, :], xT.rearrange("(k p) t -> p k t", p=P)).then_inc(s_xt, 16)
            wa = w_ada[0].rearrange("(k p) n -> p k n", p=P)
            for i in range(8):
                sp.dma_start(ada_w[i][:, :, :], wa[:, :, CHW * i:CHW * (i + 1)]).then_inc(s_ada[i], 16)
            for n in range(NCH):
                if n >= 2:
                    sp.wait_ge(s_lo, n - 1)
                sp.dma_start(chunk_view(w_raw, n), chunk_source(n)).then_inc(s_raw[n % 2], 16)
                if 0 <= n - gn - 1 < 8:
                    a = n - gn - 1
                    if a == 0:
                        sp.wait_ge(s_az, 1)
                        sp.dma_start(ada_acc[0:1, :, :].rearrange("p a n -> p (a n)"), b_ada_row).then_inc(s_ab, 16)
                        sp.wait_ge(s_ol, 8)
                    else:
                        sp.wait_ge(s_aa, 16 * a)
                    for pc in range(2):
                        col = 2 * D + CHW * (2 * a + pc)
                        sp.dma_start(ada_p[pc][:, :, :], wa[:, :, col:col + CHW]).then_inc(s_ap[pc], 16)
                if chunks[n] == ("wo", 0):
                    chunk_used(sp, n - 1)
                    sp.dma_start(x2_t[:, :, :], x.rearrange("(a p) d -> p a d", p=P)).then_inc(s_x, 16)
            sp.wait_ge(s_ml, KT)
            sp.dma_start(gffn[:, :], g_ffn.broadcast_to([P, D])).then_inc(s_gf, 16)
            sp.wait_ge(s_lo, NCH)
            sp.wait_ge(s_aa, 16 * 8)
            for c in range(3):
                expert_load(sp, 0, c)
            for tt in range(TT):
                sp.wait_ge(s_h2, 2 * tt + 2)
                sp.dma_start(h2_dram[P * tt:P * (tt + 1), :], h2_t[:, tt, :]).then_inc(s_h2w, 16)
            expert_load(sp, 0, 3)
            sp.wait_ge(s_n2, 1)
            sp.dma_start(gfin[:, :], g_final.broadcast_to([P, D])).then_inc(s_gl, 16)
            sp.wait_ge(s_lg, 1)
            expert_load(sp, 0, 4)
            sp.wait_ge(s_ix, 16 * 2 * TT)
            sp.dma_start(idx_s[:, :], idx_dram.rearrange("(p j) o -> p (j o)", p=P)).then_inc(s_il, 16)
            sp.wait_ge(s_jb, 1)
            expert_load(sp, 0, 5)
            e1 = sp.value_load(jobs_i[0:1, 1:2], min_val=0, max_val=NE - 1)
            for c in range(4):
                sp.wait_ge(s_lg2, c + 1)
                expert_load(sp, e1, c)
            before_last = sp.value_load(jobs_i[0:1, NJ:NJ + 1], min_val=14, max_val=21)
            with sp.Fori(2, before_last + 2) as i:
                e = sp.value_load(jobs_i[0:1, bass.ds(i, 1)], min_val=0, max_val=NE - 1)
                ep = sp.value_load(jobs_i[0:1, bass.ds(i - 1, 1)], min_val=0, max_val=NE - 1)
                for c in range(4):
                    sp.wait_ge(s_lg2, 4 * i + (c - 3))
                    expert_load(sp, e, c)
                for c in (4, 5):
                    sp.wait_ge(s_ld2, 2 * i + (c - 7))
                    expert_load(sp, ep, c)
            for c in (4, 5):
                sp.wait_ge(s_ld2, 2 * before_last + (c - 3))
                expert_load(sp, NE - 1, c)
            sp.wait_ge(s_ys, 16 * before_last + 48)
            for tt in range(TT):
                sp.dma_start(fin[tt][:, :, :], y_dram.rearrange("(c a p) d -> a p c d", c=2, p=P)[tt]).then_inc(s_fl[tt], 16)
            for tt in range(TT):
                sp.wait_ge(s_fo, tt + 1)
                sp.dma_start(out[P * tt:P * (tt + 1), :], fin[tt][:, 0, :]).then_inc(s_out, 16)
            sp.wait_ge(s_out, 16 * TT)

        @block.tensor
        def _(pe):
            def mm3(outap, a_hi, a_lo, b_hi, b_lo, first, last):
                pe.matmul(outap, a_hi, b_hi, start=first, stop=False)
                pe.matmul(outap, a_hi, b_lo, start=False, stop=False)
                return pe.matmul(outap, a_lo, b_hi, start=False, stop=last)

            pe.wait_ge(s_par, 16 * 5)
            for k in range(KT):
                pe.wait_ge(s_xsq, k + 1)
                mm = pe.matmul(pp[:, 0:T], mean_d, xsq[:, k, :], start=(k == 0), stop=(k == KT - 1))
            mm.then_inc(s_p0, 1)
            pe.wait_ge(s_ca, 1)
            for j in range(16):
                if j % 2 == 0:
                    pe.wait_ge(s_ada[j // 2], 16)
                for k in range(KT):
                    mm = pe.matmul(ha[:, 0, j:j + 1], ada_w[j // 2][:, k, P * (j % 2):P * (j % 2) + P],
                                   cact[:, k:k + 1], start=(k == 0), stop=(k == KT - 1))
            mm.then_inc(s_p0, 1)

            def level(qd, l):
                if l == 0:
                    for h in range(QH):
                        evacuated(pe, at_step[("q", 4 * qd + h)])
                    pe.wait_ge(s_dg, 4 * qd + 4)
                    if qd == 0:
                        pe.wait_ge(s_sq0, 1)
                    for u in range(NUNIT):
                        mm = pe.matmul(pp[:, u:u + 1], dg_t[:, u // TT, P * (u % TT):P * (u % TT) + P],
                                       ones[:, 0:1], start=True, stop=True)
                    mm.then_inc(s_lvl, 1)
                    return
                m = 1 << (l - 1)
                pe.wait_ge(s_st, 8 * qd + l)
                if l > 1:
                    pe.wait_ge(s_qu, NLEV * qd + l - 1)
                    pe.wait_ge(s_ku, NLEV * qd + l - 1)
                else:
                    pe.wait_ge(s_k, 4 * qd + 4)
                for u in range(NUNIT):
                    h, c = u // TT, u % TT
                    mm = pe.matmul(pp[:, 64 * u:64 * u + 64], k_t[:, h, P * c:P * c + P],
                                   tblk(q_t[:, h, P * c:P * c + P], m, 1), start=True, stop=True)
                mm.then_inc(s_lvl, 1)

            def quad_part(what, qd):
                if what == "x1":
                    pe.wait_ge(s_ku, NLEV * (qd + 1))
                    pe.wait_ge(s_md, 2)
                    if qd:
                        pe.wait_ge(s_rt, 1)
                    for c in range(3):
                        for h in range(QH):
                            mm = pe.transpose(ha[:, c, P * h:P * h + P], k_t[:, h, P * c:P * c + P], ident)
                    mm.then_inc(s_x1, 1)
                elif what == "x2":
                    pe.wait_ge(s_kd, qd + 1)
                    for i in range(4):
                        evacuated(pe, at_step[("iv", 4 * qd + i)])
                    for c in range(3):
                        for h in range(QH):
                            mm = pe.matmul(ha[:, c, P * h:P * h + P], kd_t[:, QH * c + h, :],
                                           v_t[:, c, DK * h:DK * h + DK], start=True, stop=True)
                    mm.then_inc(s_x2, 1)
                elif what == "x3":
                    pe.wait_ge(s_ss, 5 * (qd + 1))
                    pe.wait_ge(s_st, 8 * (qd + 1))
                    pe.wait_ge(s_qu, NLEV * (qd + 1))
                    for h in range(QH):
                        for c in range(TT):
                            o = ha[:, h, P * c:P * c + P]
                            mm = pe.matmul(o, v_t[:, c, DK * h:DK * h + DK], st_t[:, TT * h + c, :],
                                           start=True, stop=(c == 0))
                            if c:
                                mm = pe.matmul(o, ss_t[:, c - 1, DK * h:DK * h + DK],
                                               q_t[:, h, P * c:P * c + P], start=False, stop=True)
                    mm.then_inc(s_x3, 1)
                else:
                    pe.wait_ge(s_oc, 2 * (qd + 1))
                    for h in range(QH):
                        mm = pe.matmul(ha[:, h, :], mean_v, dg_t[:, h, :], start=True, stop=True)
                    mm.then_inc(s_x4, 1)

            def layernorm_part(n):
                if n == 0:
                    pe.wait_ge(s_cv, CW * CT)
                    pe.wait_ge(s_st, 16)
                else:
                    pe.wait_ge(s_la, 1)
                for ct in range(CT):
                    mm = pe.matmul(pp[:, 512 * n:512 * n + 512], mean_c, (usq if n else acc)[:, ct, :],
                                   start=(ct == 0), stop=(ct == CT - 1))
                mm.then_inc(s_l1, 1)

            def rows_part(n):
                pe.wait_ge(s_aa, 16 * 8)
                if n:
                    pe.wait_ge(s_rw, 1)
                else:
                    pe.wait_ge(s_rt, 2)
                for b in range(4):
                    mm = pe.matmul(ha[:, b, :], ones, ada_acc[:, 2 * n + b // 2, 512 * (b % 2):512 * (b % 2) + 512],
                                   start=True, stop=True)
                mm.then_inc(s_ar, 1)

            for s, (kind, tile, n, t) in enumerate(steps):
                if t == 0:
                    pe.wait_ge(s_lo, n + 1)
                if s >= 2:
                    evacuated(pe, s - 2)
                hi, lo = chunk_view(w_hi, n), chunk_view(w_lo, n)
                bank = proj[:, s % 2, :]
                if kind in ("iv", "wo"):
                    a_hi, a_lo = (h_hi, h_lo) if kind == "iv" else (m_hi, m_lo)
                    if kind == "wo" and tile == 0:
                        pe.wait_ge(s_ml, KT)
                    for j in range(2):
                        tk = slice(P * (2 * t + j), P * (2 * t + j) + P)
                        for k in range(KT):
                            mm = mm3(bank[:, CHW * j:CHW * (j + 1)], a_hi[:, k, tk], a_lo[:, k, tk],
                                     hi[:, k, :], lo[:, k, :], k == 0, k == KT - 1)
                else:
                    kk = CT if kind == "yb" else KT
                    for k in range(kk):
                        if s == 0:
                            pe.wait_ge(s_hl, k + 1)
                        if kind == "yb":
                            if tile == 0:
                                pe.wait_ge(s_cl, k + 1)
                            b_hi, b_lo = cs_hi[:, k, :], cs_lo[:, k, :]
                        elif kind == "ya":
                            if tile == 0:
                                pe.wait_ge(s_ol, k + 1)
                            b_hi, b_lo = on_hi[k // QH][:, k % QH, :], on_lo[k // QH][:, k % QH, :]
                        else:
                            b_hi, b_lo = h_hi[:, k, :], h_lo[:, k, :]
                        mm = mm3(bank, hi[:, k, P * t:P * t + P], lo[:, k, P * t:P * t + P],
                                 b_hi, b_lo, k == 0, k == kk - 1)
                mm.then_inc(s_tile, 1)
                for what in SLOT.get(s, ()):
                    if what[0] == "lev":
                        level(what[1], what[2])
                    elif what[0] == "ln":
                        layernorm_part(what[1])
                    elif what[0] == "row":
                        rows_part(what[1])
                    else:
                        quad_part(*what)

            for tt in range(TT):
                pe.wait_ge(s_h2, 2 * tt + 2)
                if tt == 0:
                    pe.wait_ge(s_rw, 2)
                if tt >= 2:
                    pe.wait_ge(s_h2c, tt - 1)
                for k in range(KT):
                    mm = pe.transpose(ha[:, 2 * (tt % 2) + k // 4, P * (k % 4):P * (k % 4) + P],
                                      h2_t[:, tt, P * k:P * k + P], ident)
                mm.then_inc(s_h2p, 1)
            for tt in range(TT):
                pe.wait_ge(s_h2c, tt + 1)
                for k in range(KT):
                    mm = pe.matmul(pp[:, NE * tt:NE * tt + NE], h2T[:, k, P * tt:P * tt + P],
                                   cols_t[:, C_WR + NE * k:C_WR + NE * k + NE],
                                   start=(k == 0), stop=(k == KT - 1))
            mm.then_inc(s_lg, 1)
            pe.wait_ge(s_dv, 1)
            for tt in range(TT):
                for t2 in range(tt + 1):
                    mm = pe.matmul(pp[:, 512 + NE * tt:512 + NE * tt + NE], tri if t2 == tt else ones,
                                   rt[:, 20, NE * t2:NE * t2 + NE], start=(t2 == 0), stop=(t2 == tt))
            for t2 in range(TT):
                mm = pe.matmul(pp[:, 576:592], ones, rt[:, 20, NE * t2:NE * t2 + NE],
                               start=(t2 == 0), stop=(t2 == TT - 1))
            mm.then_inc(s_rk, 1)

            gate_ps, up_ps = proj[:, 0, :], proj[:, 1, :]

            def tokens(i, first=False):
                pe.wait_ge(s_g, 16 * (i + 1))
                if first:
                    pe.wait_ge(s_jb, 1)
                else:
                    pe.wait_ge(s_hel, i)
                for k in range(KT):
                    mm = pe.transpose(pp[:, P * k:P * k + P], xg[:, P * k:P * k + P], ident)
                mm.then_inc(s_xp, 1)

            def half(i, c, ps):
                pe.wait_ge(s_lg2, 4 * i + c + 1)
                hi, lo = expert_view(e_hi[c], c), expert_view(e_lo[c], c)
                for k in range(4):
                    kk = 4 * (c % 2) + k
                    mm = mm3(ps, he_hi[:, P * kk:P * kk + P], he_lo[:, P * kk:P * kk + P],
                             hi[:, k, :], lo[:, k, :], kk == 0, kk == KT - 1)
                mm.then_inc(s_eu[c], 1)

            def gate(i, first=False):
                pe.wait_ge(s_hel, i + 1)
                if not first:
                    pe.wait_ge(s_sg, i)
                half(i, 0, gate_ps)
                half(i, 1, gate_ps)

            def up(i, first=False):
                if not first:
                    pe.wait_ge(s_a, i)
                half(i, 2, up_ps)
                half(i, 3, up_ps)

            def act_t(i, first=False):
                pe.wait_ge(s_a, i + 1)
                if not first:
                    pe.wait_ge(s_ael, i)
                for k in range(4):
                    mm = pe.transpose(ha[:, 0, P * k:P * k + P], a_t[:, P * k:P * k + P], ident)
                mm.then_inc(s_ad, 1)

            def down(i):
                pe.wait_ge(s_ael, i + 1)
                pe.wait_ge(s_y, i + 1)
                for c in (4, 5):
                    pe.wait_ge(s_ld2, 2 * i + c - 3)
                    hi, lo = expert_view(e_hi[c], c), expert_view(e_lo[c], c)
                    for k in range(2):
                        kk = 2 * (c - 4) + k
                        for b in range(2):
                            mm = mm3(ha[:, 1 + b, :], ae_hi[:, P * kk:P * kk + P], ae_lo[:, P * kk:P * kk + P],
                                     hi[:, k, 512 * b:512 * b + 512], lo[:, k, 512 * b:512 * b + 512],
                                     kk == 0, kk == 3)
                    mm.then_inc(s_eu[c], 1)

            tokens(0, True)
            gate(0, True)
            up(0, True)
            tokens(1)
            gate(1)
            act_t(0, True)
            up(1)
            before_last = pe.value_load(jobs_i[0:1, NJ:NJ + 1], min_val=14, max_val=21)
            with pe.Fori(2, before_last + 2) as i:
                tokens(i)
                down(i - 2)
                gate(i)
                act_t(i - 1)
                up(i)
            down(before_last)
            act_t(before_last + 1)
            down(before_last + 1)

        def raw_ready(eng, n):
            eng.wait_ge(s_raw[n % 2], 16 * (n // 2 + 1))

        def expert_raw(eng, j, c):
            eng.wait_ge(s_er[c], 16 * (j + 1))
            return e_raw[c]

        @block.scalar
        def _(act):
            act.wait_ge(s_par, 16 * 5)
            act.activation(cact[:, :], cols_t[:, C_C:C_C + 8], ACT.Sigmoid).then_inc(s_cs, 1)
            act.wait_ge(s_xt, 16)
            for k in range(KT):
                act.activation(xsq[:, k, :], xt_t[:, k, :], ACT.Square).then_inc(s_xsq, 1)
            act.wait_ge(s_eps, 1)
            act.wait_ge(s_p0, 1)
            act.activation(rst[:, :], pp[:, 0:T], ACT.Sqrt, bias=eps_c[:, 0:1]).then_inc(s_sq0, 1)

            def split_hi(n):
                raw_ready(act, n)
                if n >= 2:
                    chunk_used(act, n - 2)
                act.activation(w_hi[:, n % 2, :], w_raw[:, n % 2, :], ACT.Copy).then_inc(s_hi, 1)

            split_hi(0)
            for k in range(KT):
                act.wait_ge(s_h32, k + 1)
                act.activation(h_hi[:, k, :], xt_t[:, k, :], ACT.Copy).then_inc(s_hh, 1)

            def evacuate(s, kind, tile, n, t):
                bank = proj[:, s % 2, :]
                if kind == "cb":
                    tile_ready(act, s)
                    act.activation(acc[:, tile, :], bank, ACT.Sigmoid).then_inc(s_free[s % 2], 1)
                elif kind == "fz":
                    tile_ready(act, s)
                    if tile >= QH:
                        act.wait_ge(s_qu, 1)
                        act.wait_ge(s_ku, 1)
                        act.wait_ge(s_tot, 1)
                    act.activation(f_t[:, tile % QH, :], bank, ACT.Sigmoid).then_inc(s_free[s % 2], 1)
                elif kind in ("iv", "og"):
                    tile_ready(act, s)
                    before = [q for q in tmp_no if tmp_no[q] == tmp_no[s] - 2]
                    if before:
                        evacuated(act, before[0])
                    act.activation(tmp[:, tmp_no[s] % 2, :], bank, ACT.Sigmoid).then_inc(s_sig, 1)
                elif kind == "gb":
                    tile_ready(act, s)
                    if tile < 4:
                        act.wait_ge(s_qu, NLEV + 1)
                        act.wait_ge(s_ku, NLEV + 1)
                        act.wait_ge(s_tot, NLEV + 1)
                    else:
                        act.wait_ge(s_x1, 2)
                    act.activation(mb_t[tile // 4][:, tile % 4, :], bank, ACT.Sigmoid).then_inc(s_free[s % 2], 1)
                elif kind == "ga":
                    tile_ready(act, s)
                    if tile < 2:
                        evacuated(act, [q for q in tmp_no if tmp_no[q] == tmp_no[s] - 2][0])
                    else:
                        act.wait_ge(s_ml, tile - 1)
                    act.activation(tmp[:, tmp_no[s] % 2, :], bank, ACT.Sigmoid).then_inc(s_free[s % 2], 1)
                elif kind == "ya":
                    act.wait_ge(s_mp, tile + 1)
                    if tile == 0:
                        act.wait_ge(s_cl, CT)
                    g = at_step[("ga", tile)]
                    act.activation(m_hi[:, tile, :], tmp[:, tmp_no[g] % 2, :], ACT.Copy).then_inc(s_mh, 1)

            def o_split(qd):
                for h in range(QH):
                    act.wait_ge(s_oo, QH * qd + h + 1)
                    if qd:
                        act.wait_ge(s_x3, 2)
                    act.activation(on_hi[qd][:, h, :], o_t[:, h, :], ACT.Copy).then_inc(s_oh, 1)

            def item(what):
                if what[0] == "x1":
                    act.wait_ge(s_x1, what[1] + 1)
                    act.activation(kd_t[:, :, :].rearrange("p a b -> p (a b)"),
                                   ha[:, 0:3, :].rearrange("p a b -> p (a b)"), ACT.Copy).then_inc(s_kd, 1)
                elif what[0] == "x3":
                    act.wait_ge(s_x3, what[1] + 1)
                    act.activation(o_t[:, :, :], ha[:, :, :], ACT.Copy).then_inc(s_oc, 1)
                    act.activation(dg_t[:, :, :], ha[:, :, :], ACT.Square).then_inc(s_oc, 1)
                elif what[0] == "x4":
                    act.wait_ge(s_x4, what[1] + 1)
                    act.activation(dg_t[:, :, :], ha[:, :, :], ACT.Sqrt, bias=eps_c[:, 0:1]).then_inc(s_rt, 1)
                elif what == ("ln", 0):
                    act.wait_ge(s_ld, 1)
                    act.activation(usq[:, :, :], acc[:, :, :], ACT.Square).then_inc(s_la, 1)
                elif what == ("ln", 1):
                    act.wait_ge(s_l1, 2)
                    act.wait_ge(s_rdone, 1)
                    act.activation(rst[:, :], pp[:, 512:1024], ACT.Sqrt, bias=eps_c[:, 0:1]).then_inc(s_la, 1)
                    for ct in range(CT):
                        act.wait_ge(s_ld, 3 + ct)
                        act.activation(usq[:, ct, :], acc[:, ct, :], ACT.Identity,
                                       scale=cols_t[:, C_LG + ct:C_LG + ct + 1],
                                       bias=cols_t[:, C_LB2 + ct:C_LB2 + ct + 1]).then_inc(s_la, 1)
                        act.wait_ge(s_la, 3 + 2 * ct)
                        act.activation(acc[:, ct, :], usq[:, ct, :], ACT.Sigmoid).then_inc(s_la, 1)
                    for ct in range(CT):
                        act.wait_ge(s_cz, ct + 1)
                        if ct == 0:
                            act.wait_ge(s_p0, 1)
                        act.activation(cs_hi[:, ct, :], acc[:, ct, :], ACT.Copy).then_inc(s_ch, 1)
                elif what[0] == "row":
                    act.wait_ge(s_ar, what[1] + 1)
                    act.activation(rows[:, 2 * what[1]:2 * what[1] + 2, :].rearrange("p a (b n) -> p (a b) n", b=2),
                                   ha[:, :, :], ACT.Copy).then_inc(s_rw, 1)

            for s, (kind, tile, n, t) in enumerate(steps):
                if t == 0 and n + 1 < NCH:
                    split_hi(n + 1)
                for what in SLOT.get(s - 3, ()):
                    if what[0] == "x4":
                        o_split(what[1])
                evacuate(s, kind, tile, n, t)
                for what in SLOT.get(s, ()):
                    item(what)

            act.wait_ge(s_x2d, 8)
            act.wait_ge(s_aa, 16 * 8)
            for tt in range(TT):
                if tt:
                    act.wait_ge(s_xs, tt)
                act.activation(fsq[:, :], x2_t[:, tt, :], ACT.Square, accum_out=nst[:, tt:tt + 1]).then_inc(s_xs, 1)
            act.wait_ge(s_xs, TT)
            act.activation(nst[:, 4:8], nst[:, 0:4], ACT.Sqrt, scale=1.0 / D, bias=eps_c[:, 0:1]).then_inc(s_xs, 1)

            def esplit(j, c, first=False):
                src = expert_raw(act, j, c)
                if not first:
                    act.wait_ge(s_eu[c], j)
                act.activation(e_hi[c][:, :], src[:, :], ACT.Copy).then_inc(s_hg if c < 4 else s_hd, 1)

            act.wait_ge(s_tile, len(steps))
            for c in range(4):
                esplit(0, c, True)
            for tt in range(TT):
                act.wait_ge(s_h2p, tt + 1)
                act.activation(h2T[:, :, P * tt:P * tt + P],
                               ha[:, 2 * (tt % 2):2 * (tt % 2) + 2, :].rearrange("p a (k n) -> p (a k) n", n=P),
                               ACT.Copy).then_inc(s_h2c, 1)
            act.wait_ge(s_lg, 1)
            act.wait_ge(s_xs, TT + 1)
            act.activation(rt[:, 0, :], pp[:, 0:TT * NE], ACT.Sigmoid).then_inc(s_sc, 1)

            def silu(i, first=False):
                act.wait_ge(s_eu[1], i + 1)
                if not first:
                    act.wait_ge(s_a, i)
                act.activation(sg_t[:, :], gate_ps_(), ACT.Silu).then_inc(s_sg, 1)

            def gate_ps_():
                return proj[:, 0, :]

            def tokens_hi(i, first=False):
                act.wait_ge(s_xp, i + 1)
                if not first:
                    act.wait_ge(s_eu[3], i)
                act.activation(he_hi[:, :], pp[:, :], ACT.Copy).then_inc(s_heh, 1)

            def act_hi(i, first=False):
                act.wait_ge(s_ad, i + 1)
                if not first:
                    act.wait_ge(s_eu[5], i)
                act.activation(ae_hi[:, :], ha[:, 0, :], ACT.Copy).then_inc(s_aeh, 1)

            def body(i, second=False):
                esplit(i, 0)
                esplit(i, 1)
                silu(i - 1, second)
                tokens_hi(i)
                esplit(i, 2)
                esplit(i, 3)
                esplit(i - 1, 4, second)
                esplit(i - 1, 5, second)
                act_hi(i - 1, second)

            tokens_hi(0, True)
            act.wait_ge(s_jb, 1)
            before_last = act.value_load(jobs_i[0:1, NJ:NJ + 1], min_val=14, max_val=21)
            body(1, True)
            with act.Fori(2, before_last + 2) as i:
                body(i)
            silu(before_last + 1)
            for c in (4, 5):
                esplit(before_last + 1, c)
            act_hi(before_last + 1)

            for tt in range(TT):
                act.wait_ge(s_f2, tt + 1)
                if tt:
                    act.wait_ge(s_fa, 2 * tt - 1)
                act.activation(fsq[:, :], fin[tt][:, 1, :], ACT.Square, accum_out=nst[:, tt:tt + 1]).then_inc(s_fa, 1)
                act.wait_ge(s_fa, 2 * tt + 1)
                act.activation(nst[:, 4 + tt:5 + tt], nst[:, tt:tt + 1], ACT.Sqrt, scale=1.0 / D,
                               bias=eps_c[:, 0:1]).then_inc(s_fa, 1)

        @block.vector
        def _(dve):
            dve.memset(eps_c[:, :], EPS).then_inc(s_eps, 1)
            dve.memset(u_t[:, :, 0:PADW], 0.0).then_inc(s_pad, 1)
            dve.wait_ge(s_par, 16 * 5)
            dve.tensor_tensor(lbc[:, 0:8], cols_t[:, C_LB:C_LB + 8], cols_t[:, C_LB:C_LB + 8],
                              ALU.subtract).then_inc(s_lb, 1)
            dve.wait_ge(s_lb, 1)
            dve.tensor_scalar(lbc[:, 8:16], lbc[:, 0:8], 1.0, None, ALU.add).then_inc(s_lb, 1)
            dve.wait_ge(s_lb, 2)
            dve.tensor_tensor(lbc[:, 0:8], lbc[:, 8:16], lbc[:, 8:16], ALU.subtract).then_inc(s_lb, 1)
            dve.wait_ge(s_lb, 3)
            dve.tensor_scalar(lbc[:, 8:16], lbc[:, 0:8], -1.0, 1.0, ALU.mult, ALU.add).then_inc(s_lb, 1)
            dve.wait_ge(s_cs, 1)
            dve.tensor_tensor(cact[:, :], cact[:, :], cols_t[:, C_C:C_C + 8], ALU.mult).then_inc(s_ca, 1)
            dve.wait_ge(s_sq0, 1)
            dve.reciprocal(rst[:, :], rst[:, :]).then_inc(s_rdone0, 1)
            dve.wait_ge(s_rdone0, 1)
            dve.tensor_tensor(xt_t[:, :, :], xt_t[:, :, :],
                              rst[:, :].rearrange("p (o t) -> p o t", o=1).broadcast_to([P, KT, T]),
                              ALU.mult).then_inc(s_rdone, 1)
            dve.wait_ge(s_p0, 2)
            dve.tensor_tensor(mod1[:, :], ha[:, 0, 0:16], cols_t[:, C_BADA:C_BADA + 16], ALU.add).then_inc(s_md, 1)
            dve.wait_ge(s_md, 1)
            dve.scalar_tensor_tensor(mod1[:, 8:16], mod1[:, 8:16], 1.0, cols_t[:, C_GMIX:C_GMIX + 8],
                                     ALU.add, ALU.mult).then_inc(s_md, 1)
            dve.wait_ge(s_md, 2)
            dve.wait_ge(s_rdone, 1)
            for k in range(KT):
                dve.tensor_scalar(xt_t[:, k, :], xt_t[:, k, :], mod1[:, 8 + k:9 + k], mod1[:, k:k + 1],
                                  ALU.mult, ALU.add).then_inc(s_h32, 1)

            def split_lo(n):
                dve.wait_ge(s_hi, n + 1)
                raw_ready(dve, n)
                dve.tensor_tensor(w_lo[:, n % 2, :], w_raw[:, n % 2, :], w_hi[:, n % 2, :].bitcast(F32),
                                  ALU.subtract).then_inc(s_lo, 1)

            for k in range(KT):
                dve.wait_ge(s_hh, k + 1)
                dve.tensor_tensor(h_lo[:, k, :], xt_t[:, k, :], h_hi[:, k, :].bitcast(F32),
                                  ALU.subtract).then_inc(s_hl, 1)
                if k == 0:
                    split_lo(0)

            def evacuate(s, kind, tile, n, t):
                bank = proj[:, s % 2, :]
                free = s_free[s % 2]
                qd, h = tile // QH, tile % QH
                if kind == "ca":
                    evacuated(dve, at_step[("cb", tile)])
                    tile_ready(dve, s)
                    if tile == 0:
                        dve.wait_ge(s_pad, 1)
                    dve.tensor_tensor(u_t[:, tile, PADW:], bank, acc[:, tile, :], ALU.mult).then_inc(free, 1)
                elif kind == "fz":
                    evacuated(dve, s)
                    dve.tensor_scalar(f_t[:, h, :], f_t[:, h, :], lbc[:, 8 + tile:9 + tile],
                                      lbc[:, tile:tile + 1], ALU.mult, ALU.add).then_inc(s_fd, 1)
                elif kind == "q":
                    tile_ready(dve, s)
                    dve.wait_ge(s_k, tile + 1)
                    if qd:
                        dve.wait_ge(s_or, 5)
                        dve.wait_ge(s_x3, 1)
                    dve.scalar_tensor_tensor(dg_t[:, h, :], bank, QSCALE, k_t[:, h, :],
                                             ALU.mult, ALU.mult).then_inc(s_dg, 1)
                    dve.scalar_tensor_tensor(q_t[:, h, :], bank, QSCALE, f_t[:, h, :],
                                             ALU.mult, ALU.mult).then_inc(free, 1)
                elif kind == "iv":
                    dve.wait_ge(s_sig, tmp_no2[s] + 1)
                    if qd:
                        dve.wait_ge(s_x3, 1)
                    c0 = CHW * ((tile // 2) % 2)
                    dve.tensor_tensor(v_t[:, 2 * t:2 * t + 2, c0:c0 + CHW],
                                      bank.rearrange("p (a n) -> p a n", a=2),
                                      tmp[:, tmp_no[s] % 2, :].rearrange("p (a n) -> p a n", a=2),
                                      ALU.mult).then_inc(free, 1)
                elif kind == "og":
                    dve.wait_ge(s_sig, tmp_no2[s] + 1)
                    if qd:
                        dve.wait_ge(s_oo, 4)
                    dve.tensor_tensor(og_t[:, h, :], bank, tmp[:, tmp_no[s] % 2, :], ALU.mult).then_inc(free, 1)
                elif kind == "yb":
                    tile_ready(dve, s)
                    evacuated(dve, at_step[("gb", tile)])
                    m = mb_t[tile // 4][:, tile % 4, :]
                    dve.tensor_tensor(m, bank, m, ALU.mult).then_inc(free, 1)
                elif kind == "ya":
                    g = at_step[("ga", tile)]
                    tile_ready(dve, s)
                    evacuated(dve, g)
                    sl = tmp[:, tmp_no[g] % 2, :]
                    dve.tensor_tensor(sl, bank, sl, ALU.mult).then_inc(free, 1)
                    dve.wait_ge(s_mh, tile + 1)
                    dve.tensor_tensor(m_lo[:, tile, :], sl, m_hi[:, tile, :].bitcast(F32),
                                      ALU.subtract).then_inc(s_ml, 1)
                elif kind == "wo":
                    tile_ready(dve, s)
                    if tile == 0:
                        dve.wait_ge(s_rw, 1)
                        dve.wait_ge(s_x, 16)
                    else:
                        dve.wait_ge(s_x2d, tile)
                    c0 = CHW * (tile // 2)
                    r2 = rst[:, :].rearrange("p (a n) -> p a n", a=2)
                    dve.tensor_tensor(r2, bank.rearrange("p (a n) -> p a n", a=2),
                                      rows[:, 0:1, c0:c0 + CHW].broadcast_to([P, 2, CHW]), ALU.mult).then_inc(free, 1)
                    evacuated(dve, s)
                    xs = x2_t[:, 2 * t:2 * t + 2, c0:c0 + CHW]
                    dve.tensor_tensor(xs, xs, r2, ALU.add).then_inc(s_x2d, 1)

            conv_at = [0]

            def conv(upto):
                while conv_at[0] < min(upto, CW * CT):
                    i = conv_at[0]
                    w, ct = i // CT, i % CT
                    src = u_t[:, ct, w:w + T]
                    tap = cols_t[:, C_CW + CW * ct + w:C_CW + CW * ct + w + 1]
                    if w == 0:
                        evacuated(dve, at_step[("ca", ct)])
                        dve.tensor_scalar(acc[:, ct, :], src, tap, cols_t[:, C_CB + ct:C_CB + ct + 1],
                                          ALU.mult, ALU.add).then_inc(s_cv, 1)
                    else:
                        dve.wait_ge(s_cv, i - CT + 1)
                        dve.scalar_tensor_tensor(acc[:, ct, :], src, tap, acc[:, ct, :],
                                                 ALU.mult, ALU.add).then_inc(s_cv, 1)
                    conv_at[0] += 1

            def item(what):
                if what[0] == "lev" and what[2] == 0:
                    qd = what[1]
                    dve.wait_ge(s_lvl, 8 * qd + 1)
                    if qd:
                        dve.wait_ge(s_ol, 4)
                    dve.tensor_tensor(st_t[:, :, :], ident.rearrange("p (o n) -> p o n", o=1).broadcast_to([P, NUNIT, P]),
                                      pp[:, 0:NUNIT].rearrange("p (u o) -> p u o", o=1).broadcast_to([P, NUNIT, P]),
                                      ALU.mult).then_inc(s_st, 1)
                elif what[0] == "lev":
                    qd, l = what[1], what[2]
                    m = 1 << (l - 1)
                    dve.wait_ge(s_lvl, 8 * qd + l + 1)
                    dve.wait_ge(s_st, 8 * qd + l)
                    dst = st_t[:, :, :].rearrange("p u (b two m) -> p u b two m", two=2, m=m)[:, :, :, 1, :]
                    msk = mask_t[:, 64 * (l - 1):64 * l].rearrange("p (o b m) -> p o b m", o=1, m=m)
                    dve.copy_predicated(dst, msk.broadcast_to([P, NUNIT, 64 // m, m]),
                                        pp[:, :].rearrange("p (u b m) -> p u b m", u=NUNIT, m=m)).then_inc(s_st, 1)
                    if l == 1:
                        dve.wait_ge(s_fd, 4 * qd + 4)
                    else:
                        dve.wait_ge(s_tot, NLEV * qd + l - 1)
                        dve.wait_ge(s_qu, NLEV * qd + l - 1)
                    qv = tblk(q_t[:, :, :].rearrange("p h t -> p (h t)"), m, 1)
                    tv = flat(tot[l - 1]).rearrange("p (b two) -> p b two", two=2)[:, :, 0:1]
                    dve.tensor_tensor(qv, qv, tv.broadcast_to([P, 1024 // m, m]), ALU.mult).then_inc(s_qu, 1)
                elif what[0] == "x2":
                    qd = what[1]
                    dve.wait_ge(s_x2, qd + 1)
                    dve.tensor_copy(ss_t[:, 0, :], ha[:, 0, :]).then_inc(s_ss, 1)
                    for c in (1, 2):
                        dec = tot[NLEV][:, :].rearrange("p (h c) -> p h c", c=TT)[:, :, c:c + 1]
                        dve.wait_ge(s_ss, 5 * qd + 2 * c - 1)
                        dve.tensor_tensor(ss_t[:, c, :].rearrange("p (h n) -> p h n", h=QH),
                                          ss_t[:, c - 1, :].rearrange("p (h n) -> p h n", h=QH),
                                          dec.broadcast_to([P, QH, DK]), ALU.mult).then_inc(s_ss, 1)
                        dve.wait_ge(s_ss, 5 * qd + 2 * c)
                        dve.tensor_tensor(ss_t[:, c, :], ss_t[:, c, :], ha[:, c, :], ALU.add).then_inc(s_ss, 1)
                elif what[0] == "x4":
                    qd = what[1]
                    dve.wait_ge(s_rt, qd + 1)
                    dve.reciprocal(dg_t[:, :, :], dg_t[:, :, :]).then_inc(s_or, 1)
                    dve.wait_ge(s_or, 5 * qd + 1)
                    for h in range(QH):
                        g = cols_t[:, C_ON + 4 * qd + h:C_ON + 4 * qd + h + 1]
                        dve.scalar_tensor_tensor(o_t[:, h, :], o_t[:, h, :], g, dg_t[:, h, :],
                                                 ALU.mult, ALU.mult).then_inc(s_or, 1)
                elif what == ("ln", 0):
                    dve.wait_ge(s_l1, 1)
                    dve.tensor_tensor(acc[:, :, :], acc[:, :, :],
                                      pp[:, 0:T].rearrange("p (o t) -> p o t", o=1).broadcast_to([P, CT, T]),
                                      ALU.subtract).then_inc(s_ld, 1)
                elif what == ("ln", 1):
                    dve.wait_ge(s_la, 2)
                    dve.reciprocal(rst[:, :], rst[:, :]).then_inc(s_ld, 1)
                    dve.wait_ge(s_ld, 2)
                    for ct in range(CT):
                        dve.tensor_tensor(acc[:, ct, :], acc[:, ct, :], rst[:, :], ALU.mult).then_inc(s_ld, 1)
                    for ct in range(CT):
                        dve.wait_ge(s_la, 4 + 2 * ct)
                        dve.tensor_tensor(acc[:, ct, :], acc[:, ct, :], usq[:, ct, :], ALU.mult).then_inc(s_cz, 1)
                    for ct in range(CT):
                        dve.wait_ge(s_ch, ct + 1)
                        dve.tensor_tensor(cs_lo[:, ct, :], acc[:, ct, :], cs_hi[:, ct, :].bitcast(F32),
                                          ALU.subtract).then_inc(s_cl, 1)

            def o_lo(qd):
                for h in range(QH):
                    dve.wait_ge(s_oh, QH * qd + h + 1)
                    dve.tensor_tensor(on_lo[qd][:, h, :], o_t[:, h, :], on_hi[qd][:, h, :].bitcast(F32),
                                      ALU.subtract).then_inc(s_ol, 1)

            def ada_piece_pair(a):
                for k in range(KT):
                    for pc in range(2):
                        col = CHW * (2 * a + pc)
                        dst = ada_acc[:, col // D, col % D:col % D + CHW]
                        if k == 0:
                            dve.wait_ge(s_ap[pc], 16 * (a + 1))
                            if a == 0:
                                dve.wait_ge(s_ab, 16)
                        else:
                            dve.wait_ge(s_aa, 16 * a + 2 * k - 1 + pc)
                        dve.scalar_tensor_tensor(dst, ada_p[pc][:, k, :], cact[:, k:k + 1], dst,
                                                 ALU.mult, ALU.add).then_inc(s_aa, 1)

            first_conv = at_step[("ca", 3)] + 1
            last_conv = 39
            for s, (kind, tile, n, t) in enumerate(steps):
                if n == gn and t == 0:
                    chunk_used(dve, gn - 1)
                    dve.memset(ada_acc[:, :, :], 0.0).then_inc(s_az, 1)
                if t == 0 and n + 1 < NCH:
                    split_lo(n + 1)
                evacuate(s, kind, tile, n, t)
                for what in SLOT.get(s, ()):
                    item(what)
                for what in SLOT.get(s - 3, ()):
                    if what[0] == "x4":
                        o_lo(what[1])
                if first_conv <= s <= last_conv:
                    conv(-(-CW * CT * (s - first_conv + 1) // (last_conv - first_conv + 1)))
                if gn <= n < gn + 8 and t == 1:
                    ada_piece_pair(n - gn)

            dve.wait_ge(s_rw, 2)
            dve.wait_ge(s_gf, 16)
            dve.scalar_tensor_tensor(rows[:, 2, :], rows[:, 2, :], 1.0, gffn[:, :], ALU.add, ALU.mult).then_inc(s_n2, 1)
            dve.wait_ge(s_xs, TT + 1)
            dve.reciprocal(nst[:, 4:8], nst[:, 4:8]).then_inc(s_n2, 1)
            dve.wait_ge(s_n2, 2)
            dve.wait_ge(s_mp, KT)
            for tt in range(TT):
                dve.scalar_tensor_tensor(h2_t[:, tt, :], x2_t[:, tt, :], nst[:, 4 + tt:5 + tt], rows[:, 2, :],
                                         ALU.mult, ALU.mult).then_inc(s_h2, 1)
                dve.wait_ge(s_h2, 2 * tt + 1)
                dve.tensor_tensor(h2_t[:, tt, :], h2_t[:, tt, :], rows[:, 1, :], ALU.add).then_inc(s_h2, 1)

            def elo(i, c, first=False):
                src = expert_raw(dve, i, c)
                dve.wait_ge(s_hg, 4 * i + c + 1)
                dve.tensor_tensor(e_lo[c][:, :], src[:, :], e_hi[c][:, :].bitcast(F32),
                                  ALU.subtract).then_inc(s_lg2, 1)

            for c in range(3):
                elo(0, c)

            n_r = [0]

            def step(ins, also=None):
                n_r[0] += 1
                ins.then_inc(s_r, 1)
                dve.wait_ge(s_r, n_r[0])

            def r(i, a=0, b=TT * NE):
                return rt[:, i, a:b]

            def four(ap):
                return ap.rearrange("p (g e) -> p g e", e=4)

            def col(ap):
                return ap.rearrange("p (g o) -> p g o", o=1)

            def tt_(o, a, b, op):
                step(dve.tensor_tensor(o, a, b, op))

            def first_of_four(dst, src, run):
                step(dve.tensor_copy(run, src[:, :, 0:1]))
                step(dve.tensor_copy(dst[:, :, 0:1], src[:, :, 0:1]))
                for e in range(1, 4):
                    tt_(dst[:, :, e:e + 1], src[:, :, e:e + 1], run, ALU.is_gt)
                    if e < 3:
                        tt_(run, run, src[:, :, e:e + 1], ALU.max)

            dve.wait_ge(s_sc, 1)
            by_tt = lambda ap: ap.rearrange("p (a e) -> p a e", a=TT)
            tt_(by_tt(r(1)), by_tt(r(0)), rb_t[:, :].rearrange("p (o e) -> p o e", o=1).broadcast_to([P, TT, NE]), ALU.add)
            v = four(r(1))
            q1, q2, q3, q4 = [(16 * a, 16 * a + 16) for a in range(4)]
            tt_(col(r(2, *q1)), v[:, :, 0:1], v[:, :, 1:2], ALU.max)
            tt_(col(r(2, *q2)), v[:, :, 0:1], v[:, :, 1:2], ALU.min)
            tt_(col(r(2, *q3)), v[:, :, 2:3], v[:, :, 3:4], ALU.max)
            tt_(col(r(2, *q4)), v[:, :, 2:3], v[:, :, 3:4], ALU.min)
            tt_(r(3, *q1), r(2, *q1), r(2, *q3), ALU.max)
            tt_(r(3, *q2), r(2, *q1), r(2, *q3), ALU.min)
            tt_(r(3, *q3), r(2, *q2), r(2, *q4), ALU.max)
            tt_(r(3, *q4), r(3, *q2), r(3, *q3), ALU.max)
            tt_(r(4, *q1), r(3, *q1), r(3, *q4), ALU.add)
            step(dve.tensor_reduce(r(5, 0, 4), four(r(4, *q1)), AX.X, ALU.max))
            tt_(four(r(6, *q1)), four(r(4, *q1)), col(r(5, 0, 4)).broadcast_to([P, 4, 4]), ALU.is_equal)
            first_of_four(four(r(7, *q1)), four(r(6, *q1)), col(r(5, 8, 12)))
            tt_(four(r(8)), v, col(r(3, *q1)).broadcast_to([P, 16, 4]), ALU.is_equal)
            first_of_four(four(r(9)), four(r(8)), col(r(5, 16, 32)))
            tt_(four(r(10)), v, col(r(3, *q4)).broadcast_to([P, 16, 4]), ALU.is_equal)
            tt_(r(11), r(10), r(9), ALU.is_gt)
            first_of_four(four(r(12)), four(r(11)), col(r(5, 16, 32)))
            gsel = col(r(7, *q1)).broadcast_to([P, 16, 4])
            tt_(four(r(13)), four(r(9)), gsel, ALU.mult)
            tt_(four(r(14)), four(r(12)), gsel, ALU.mult)
            dve.tensor_tensor(r(20), r(13), r(14), ALU.add).then_inc(s_dv, 1)
            tt_(r(15), r(0), r(13), ALU.mult)
            tt_(r(16), r(0), r(14), ALU.mult)
            step(dve.tensor_reduce(wsel[:, 0, :], by_tt(r(15)), AX.X, ALU.add))
            step(dve.tensor_reduce(wsel[:, 1, :], by_tt(r(16)), AX.X, ALU.add))
            tt_(r(5, 40, 44), wsel[:, 0, :], wsel[:, 1, :], ALU.add)
            step(dve.reciprocal(r(5, 44, 48), r(5, 40, 44)))
            tt_(wsel[:, 0, :], wsel[:, 0, :], r(5, 44, 48), ALU.mult)
            tt_(wsel[:, 1, :], wsel[:, 1, :], r(5, 44, 48), ALU.mult)
            step(dve.memset(r(19, 0, 16), 0.0))
            dve.wait_ge(s_rk, 1)
            rank, cnt = r(21), r(22, 0, 16)
            step(dve.tensor_copy(rank, pp[:, 512:576]))
            step(dve.tensor_copy(cnt, pp[:, 576:592]))
            nb, incl, start = r(23, 0, 16), r(23, 16, 32), r(23, 32, 48)
            step(dve.tensor_scalar(nb, cnt, float(P), 1.0, ALU.is_gt, ALU.add))
            for b in (2, 3):
                step(dve.scalar_tensor_tensor(nb, cnt, float(P * b), nb, ALU.is_gt, ALU.add))
            step(dve.tensor_tensor_scan(incl, nb, r(19, 0, 16), 0.0, ALU.add, ALU.add))
            tt_(start, incl, nb, ALU.subtract)
            step(dve.tensor_scalar(r(24), rank, float(P), None, ALU.is_ge))
            for b in (2, 3):
                step(dve.scalar_tensor_tensor(r(24), rank, float(P * b), r(24), ALU.is_ge, ALU.add))
            step(dve.scalar_tensor_tensor(by_tt(r(25)), by_tt(rank), float(NJ),
                                          start.rearrange("p (o e) -> p o e", o=1).broadcast_to([P, TT, NE]),
                                          ALU.mult, ALU.add))
            step(dve.scalar_tensor_tensor(r(25), r(24), float(1 - P * NJ), r(25), ALU.mult, ALU.add))
            for c in range(2):
                tt_(r(26 + c), r(13 + c), r(25), ALU.mult)
                step(dve.tensor_reduce(r(19, 16 + 4 * c, 20 + 4 * c), by_tt(r(26 + c)), AX.X, ALU.add))
            dve.tensor_copy(pos_i[:, :], r(19, 16, 24)).then_inc(s_ps, 1)
            ge = rt[:, 26:32, :].rearrange("p a b -> p (a b)").rearrange("p (j e) -> p j e", e=NE)
            tt_(ge, con_t[:, K_JI:K_JI + NJ].rearrange("p (j o) -> p j o", o=1).broadcast_to([P, NJ, NE]),
                start.rearrange("p (o e) -> p o e", o=1).broadcast_to([P, NJ, NE]), ALU.is_ge)
            step(dve.tensor_reduce(r(18, 0, NJ), ge, AX.X, ALU.add))
            step(dve.tensor_scalar(r(18, 32, 32 + NJ), r(18, 0, NJ), -1.0, None, ALU.add))
            step(dve.tensor_copy(jobs_i[:, 0:NJ], r(18, 32, 32 + NJ)))
            dve.tensor_scalar(jobs_i[:, NJ:NJ + 1], incl[:, NE - 1:NE], -2.0, None, ALU.add).then_inc(s_jb, 1)
            dve.wait_ge(s_il, 16)
            dve.tensor_single_scalar(idx_g[:, :], idx_s[:, :], T - 1, ALU.bitwise_and).then_inc(s_ig, 1)
            dve.memset(nst[:, 0:1], 0.0).then_inc(s_y, 1)
            elo(0, 3)

            def tokens_lo(i):
                dve.wait_ge(s_heh, i + 1)
                dve.tensor_tensor(he_lo[:, :], pp[:, :], he_hi[:, :].bitcast(F32), ALU.subtract).then_inc(s_hel, 1)

            def product(i, first=False):
                dve.wait_ge(s_sg, i + 1)
                dve.wait_ge(s_eu[3], i + 1)
                if not first:
                    dve.wait_ge(s_ad, i)
                dve.tensor_tensor(a_t[:, :], proj[:, 1, :], sg_t[:, :], ALU.mult).then_inc(s_a, 1)

            def act_lo(i):
                dve.wait_ge(s_aeh, i + 1)
                dve.tensor_tensor(ae_lo[:, :], ha[:, 0, :], ae_hi[:, :].bitcast(F32), ALU.subtract).then_inc(s_ael, 1)

            def y_out(i):
                dve.wait_ge(s_eu[5], i + 1)
                dve.wait_ge(s_ys, 16 * (i + 1))
                dve.tensor_tensor(y_sb[:, :], ha[:, 1:3, :].rearrange("p a n -> p (a n)"), rows[:, 3, :],
                                  ALU.mult).then_inc(s_y, 1)

            def body(i, second=False):
                elo(i, 0)
                elo(i, 1)
                product(i - 1, second)
                tokens_lo(i)
                elo(i, 2)
                elo(i, 3)
                if not second:
                    y_out(i - 2)
                act_lo(i - 1)

            tokens_lo(0)
            before_last = dve.value_load(jobs_i[0:1, NJ:NJ + 1], min_val=14, max_val=21)
            body(1, True)
            with dve.Fori(2, before_last + 2) as i:
                body(i)
            product(before_last + 1)
            y_out(before_last)
            act_lo(before_last + 1)
            y_out(before_last + 1)

            for tt in range(TT):
                dve.wait_ge(s_fl[tt], 16)
                dve.scalar_tensor_tensor(fin[tt][:, 0, :], fin[tt][:, 0, :], wsel[:, 0, tt:tt + 1], x2_t[:, tt, :],
                                         ALU.mult, ALU.add).then_inc(s_f1, 1)
                dve.wait_ge(s_f1, tt + 1)
                dve.scalar_tensor_tensor(fin[tt][:, 1, :], fin[tt][:, 1, :], wsel[:, 1, tt:tt + 1], fin[tt][:, 0, :],
                                         ALU.mult, ALU.add).then_inc(s_f2, 1)
            dve.wait_ge(s_gl, 16)
            for tt in range(TT):
                dve.wait_ge(s_fa, 2 * tt + 2)
                dve.reciprocal(nst[:, 4 + tt:5 + tt], nst[:, 4 + tt:5 + tt]).then_inc(s_fr, 1)
                dve.wait_ge(s_fr, tt + 1)
                dve.wait_ge(s_f2, tt + 1)
                dve.scalar_tensor_tensor(fin[tt][:, 0, :], fin[tt][:, 1, :], nst[:, 4 + tt:5 + tt], gfin[:, :],
                                         ALU.mult, ALU.mult).then_inc(s_fo, 1)

        @block.gpsimd
        def _(pool):
            pool.memset(idx_s[:, :], PADIDX).then_inc(s_pf, 1)
            pool.wait_ge(s_pf, 1)
            pool.dma_start(idx_dram.rearrange("(p j) o -> p (j o)", p=P), idx_s[:, :]).then_inc(s_ys, 16)

            def totals(qd):
                pool.wait_ge(s_fd, 4 * qd + 4)
                if qd:
                    pool.wait_ge(s_x2, 1)
                    pool.wait_ge(s_ss, 5)
                for l in range(1, NLEV + 1):
                    src = flat(tot[l - 1]).rearrange("p (b two) -> p b two", two=2)
                    if l > 1:
                        pool.wait_ge(s_tot, NLEV * qd + l - 1)
                    pool.tensor_tensor(flat(tot[l]).rearrange("p (b o) -> p b o", o=1), src[:, :, 0:1], src[:, :, 1:2],
                                       ALU.mult).then_inc(s_tot, 1)

            for s, (kind, tile, n, t) in enumerate(steps):
                if kind == "fz":
                    pool.wait_ge(s_fd, tile + 1)
                    if tile >= QH:
                        pool.wait_ge(s_x1, 1)
                    pool.tensor_scalar(k_t[:, tile % QH, :], f_t[:, tile % QH, :], -1.0, 1.0,
                                       ALU.mult, ALU.add).then_inc(s_k, 1)
                    if tile % QH == QH - 1:
                        totals(tile // QH)
                elif kind == "ya":
                    evacuated(pool, s)
                    evacuated(pool, at_step[("yb", tile)])
                    sl = tmp[:, tmp_no[at_step[("ga", tile)]] % 2, :]
                    pool.tensor_tensor(sl, sl, mb_t[tile // 4][:, tile % 4, :], ALU.add).then_inc(s_mp, 1)
                for what in SLOT.get(s, ()):
                    if what[0] == "lev" and what[2] > 0:
                        qd, l = what[1], what[2]
                        m = 1 << (l - 1)
                        pool.wait_ge(s_lvl, 8 * qd + l + 1)
                        if l > 1:
                            pool.wait_ge(s_ku, NLEV * qd + l - 1)
                            pool.wait_ge(s_tot, NLEV * qd + l - 1)
                        else:
                            pool.wait_ge(s_k, 4 * qd + 4)
                        kv = tblk(k_t[:, :, :].rearrange("p h t -> p (h t)"), m, 0)
                        tv = flat(tot[l - 1]).rearrange("p (b two) -> p b two", two=2)[:, :, 1:2]
                        pool.tensor_tensor(kv, kv, tv.broadcast_to([P, 1024 // m, m]), ALU.mult).then_inc(s_ku, 1)
                    elif what[0] == "x4":
                        qd = what[1]
                        for h in range(QH):
                            evacuated(pool, at_step[("og", 4 * qd + h)])
                            pool.wait_ge(s_or, 5 * qd + h + 2)
                            pool.tensor_tensor(o_t[:, h, :], o_t[:, h, :], og_t[:, h, :], ALU.mult).then_inc(s_oo, 1)

            pool.wait_ge(s_ys, 16)
            pool.wait_ge(s_ps, 1)
            pool.wait_ge(s_par, 16 * 5)
            for c in range(2 * TT):
                pool.indirect_dma_start(idx_dram, bass.IndirectOffsetOnAxis(ap=pos_i[:, c:c + 1], axis=0),
                                        vals_t[:, c:c + 1], None).then_inc(s_ix, 16)

            def gather(i, first=False):
                if not first:
                    pool.wait_ge(s_xp, i)
                    pool.wait_ge(s_g, 16 * i)
                pool.tensor_copy(gi[:, :], idx_g[:, bass.ds(i, 1)]).then_inc(s_gc, 1)
                pool.wait_ge(s_gc, i + 1)
                pool.wait_ge(s_sp[0], i + 1)
                pool.tensor_tensor(spacer[0][:, :], ones[:, 0:1], ones[:, 0:1], ALU.mult).then_inc(s_sp[0], 1)
                pool.indirect_dma_start(xg[:, :], None, h2_dram,
                                        bass.IndirectOffsetOnAxis(ap=gi[:, 0:1], axis=0)).then_inc(s_g, 16)

            def scatter(i):
                pool.wait_ge(s_ys, 16 * (i + 1))
                pool.tensor_copy(si[:, :], idx_s[:, bass.ds(i, 1)]).then_inc(s_yc, 1)
                pool.wait_ge(s_yc, i + 1)
                pool.wait_ge(s_y, i + 2)
                pool.wait_ge(s_sp[1], i + 1)
                pool.tensor_tensor(spacer[1][:, :], ones[:, 0:1], ones[:, 0:1], ALU.mult).then_inc(s_sp[1], 1)
                pool.indirect_dma_start(y_dram, bass.IndirectOffsetOnAxis(ap=si[:, 0:1], axis=0), y_sb[:, :], None,
                                        bounds_check=NPAIR - 1, oob_is_err=False).then_inc(s_ys, 16)

            def down_lo(j):
                for c in (4, 5):
                    src = expert_raw(pool, j, c)
                    pool.wait_ge(s_hd, 2 * j + c - 3)
                    pool.tensor_tensor(e_lo[c][:, :], src[:, :], e_hi[c][:, :].bitcast(F32),
                                       ALU.subtract).then_inc(s_ld2, 1)

            for sp_ in range(2):
                pool.tensor_tensor(spacer[sp_][:, :], ones[:, 0:1], ones[:, 0:1], ALU.mult).then_inc(s_sp[sp_], 1)
            pool.wait_ge(s_ig, 1)
            pool.wait_ge(s_h2w, 16 * TT)
            pool.wait_ge(s_h2p, TT)
            before_last = pool.value_load(jobs_i[0:1, NJ:NJ + 1], min_val=14, max_val=21)
            gather(0, True)
            gather(1)
            gather(2)
            down_lo(0)
            with pool.Fori(2, before_last + 2) as i:
                gather(i + 1)
                down_lo(i - 1)
                scatter(i - 2)
            down_lo(before_last + 1)
            scatter(before_last)
            scatter(before_last + 1)
            pool.wait_ge(s_g, 16 * before_last + 48)


def kernel(**inputs):
    import concourse.bacc as _bacc
    from concourse.bass_utils import run_bass_kernel_spmd as _run

    a = {k: np.ascontiguousarray(v) for k, v in inputs.items()}

    def per_channel(v):
        return v.reshape(-1, P).T

    cols = np.concatenate([
        per_channel(a["c"]), per_channel(a["b_ada"][0, :2 * D]), per_channel(a["norm_mix_g"]),
        per_channel(a["hgrn_lb_logits"][0]), per_channel(a["hgrn_onorm_g"]),
        a["conv_w"][0].T.reshape(CT, P, CW).transpose(1, 0, 2).reshape(P, CT * CW),
        per_channel(a["conv_b"]), per_channel(a["conv_ln_g"]), per_channel(a["conv_ln_b"]),
        a["w_router"].reshape(KT, P, NE).transpose(1, 0, 2).reshape(P, KT * NE)], axis=1)
    one = np.ones((P, P), np.float32)
    consts = np.concatenate([np.eye(P, dtype=np.float32), one, one / D, one / CC, one / DK,
                             np.triu(one, 1), np.tile(np.arange(NJ, dtype=np.float32), (P, 1))], axis=1)
    s = np.arange(P)
    masks = []
    for l in range(NLEV):
        m = 1 << l
        t = np.array([b * 2 * m + m + j for b in range(64 // m) for j in range(m)])
        masks.append((s[:, None] // (2 * m) == t[None, :] // (2 * m)) & (s[:, None] % (2 * m) < m))
    masks = np.concatenate(masks, axis=1).astype(np.int32)
    vals = (s[:, None] + np.array([c * T + tt * P for c in range(2) for tt in range(TT)])[None, :]).astype(np.int32)

    feed = {
        "xT": a["x"][0].T, "x": a["x"][0], "cols": cols, "consts": consts, "masks": masks, "vals": vals,
        "w_ada": a["w_ada"], "b_ada_row": a["b_ada"][:, 2 * D:], "w_in": a["w_in"],
        "w_o_hgrn": a["w_o_hgrn"], "w_o_conv": a["w_o_conv"], "w_out": a["w_out"],
        "router_bias": a["router_bias"].reshape(1, NE), "g_ffn": a["norm_ffn_g"].reshape(1, D),
        "g_final": a["final_norm_g"].reshape(1, D),
        "w_gate": a["w_gate_e"], "w_up": a["w_up_e"], "w_down": a["w_down_e"],
    }
    nc = _bacc.Bacc("TRN2", target_bir_lowering=False, num_devices=1)
    arrays, args = {}, []
    for name, v in feed.items():
        v = np.ascontiguousarray(v)
        arrays[f"in_{name}"] = v
        args.append(nc.dram_tensor(f"in_{name}", v.shape, mybir.dt.from_np(v.dtype), kind="ExternalInput").ap())
    args.append(nc.dram_tensor("h2_rows", (T, D), F32, kind="Internal").ap())
    args.append(nc.dram_tensor("y_rows", (NPAIR, D), F32, kind="Internal").ap())
    args.append(nc.dram_tensor("index_table", (P * NJ, 1), I32, kind="Internal").ap())
    args.append(nc.dram_tensor("out_0", (T, D), F32, kind="ExternalOutput").ap())
    trunk_kernel(nc, *args)
    r = _run(nc, [arrays], core_ids=[0])
    return r.results[0]["out_0"].reshape(1, T, D)
```

```python
from contextlib import ExitStack

import concourse.bass as bass
from concourse import mybir
import numpy as np

F32 = mybir.dt.float32
F32R = mybir.dt.float32r
I32 = mybir.dt.int32
ACT = mybir.ActivationFunctionType
ALU = mybir.AluOpType
AX = mybir.AxisListType

P = 128
T = 512
D = 1024
KT = D // P
TT = T // P
QH = 4
DK = 128
QSCALE = DK ** -0.5
CC = 512
CT = CC // P
CW = 31
PADW = CW - 1
NE = 16
FF = 512
EPS = 1e-6
CHW = 256
NUNIT = QH * TT
NLEV = 7
NJ = 24
NPAIR = 2 * T
PADIDX = 1 << 14

C_C, C_BADA, C_GMIX, C_LB, C_ON = 0, 8, 24, 32, 40
C_CW, C_CB, C_LG, C_LB2, C_WR = 48, 48 + CT * CW, 52 + CT * CW, 56 + CT * CW, 60 + CT * CW
C_ALL = C_WR + KT * NE
K_ID, K_ONE, K_MD, K_MC, K_MV, K_TRI, K_IO = 0, 128, 256, 384, 512, 640, 768
K_W4, K_VAL = K_IO + P, K_IO + P + 4
K_ALL = K_VAL + 2 * TT


ADA_DVE = (4, 1, 2, 3, 7)


def plan():
    chunks = [("cb", i) for i in range(2)] + [("ca", i) for i in range(2)]
    for qd in range(2):
        chunks += [(k, 2 * qd + i) for k in ("fz", "q", "iv", "og") for i in range(2)]
    chunks += [("gb", i) for i in range(4)] + [("yb", i) for i in range(2)]
    for i in range(4):
        chunks += [("ga", i), ("ya", i)]
    chunks += [("wo", i) for i in range(4)]
    steps = []
    for n, (kind, i) in enumerate(chunks):
        for t in range(4 if kind == "yb" else 2):
            steps.append((kind, (4 if kind == "yb" else 2) * i + t, n, t))
    return chunks, steps


def trunk_kernel(nc, xT, x, cols, consts, masks, w_ada, b_ada_row, w_in, w_o_hgrn, w_o_conv,
                 w_out, router_bias, g_ffn, g_final, w_gate, w_up, w_down, h2_dram, y_dram,
                 out):
    chunks, steps = plan()
    at_step = {}
    for s, (kind, tile, _, _) in enumerate(steps):
        at_step[(kind, tile)] = s
    tmp_no = {}
    for s, (kind, tile, _, _) in enumerate(steps):
        if kind in ("iv", "og", "ga"):
            tmp_no[s] = len(tmp_no)

    sigs = [s for s, (kind, _, _, _) in enumerate(steps) if kind in ("iv", "og")]
    tmp_no2 = {s: n for n, s in enumerate(sigs)}

    ctx = ExitStack()
    with ctx:
        base = (nc.sbuf_base + 63) // 64 * 64
        top = [base]
        placed = {}

        def region(name, nbytes):
            placed[name] = top[0]
            top[0] += (nbytes + 63) // 64 * 64
            assert top[0] <= nc.sbuf_usable_end, (name, top[0])

        def at(name, where, shape, dt=F32, plus=0):
            return nc.alloc_sbuf_tensor_at(name, shape, dt, offset=placed[where] + plus)

        for r, n in (("HT", 32768), ("WRAW", 16384), ("WS", 32768), ("F", 8192), ("K", 8192),
                     ("Q", 8192), ("V", 8192), ("TOT", 8192), ("OG", 8192), ("DG", 8192),
                     ("ST", 8192), ("UACC", 4 * CT * (T + PADW) + 8192), ("CS", 16384),
                     ("ON0", 16384), ("COLS", 4 * C_ALL), ("CONST", 4 * K_ALL),
                     ("MASK", 4 * NLEV * 64), ("TMP", 4096), ("RST", 2048), ("SMALL", 1024)):
            region(r, n)

        h_hi = at("h_hi", "HT", [P, KT, T], F32R)
        h_lo = at("h_lo", "HT", [P, KT, T], F32R, 16384)
        w_raw = at("w_raw", "WRAW", [P, 2, 2048])
        w_hi = at("w_hi", "WS", [P, 2, 2048], F32R)
        w_lo = at("w_lo", "WS", [P, 2, 2048], F32R, 16384)
        f_t = at("f_t", "F", [P, QH, T])
        k_t = at("k_t", "K", [P, QH, T])
        q_t = at("q_t", "Q", [P, QH, T])
        v_t = at("v_t", "V", [P, TT, QH * DK])
        og_t = at("og_t", "OG", [P, QH, T])
        dg_t = at("dg_t", "DG", [P, QH, T])
        osq = at("osq", "V", [P, QH, T])
        st_t = at("st_t", "ST", [P, NUNIT, P])
        o_t = at("o_t", "ST", [P, QH, T])
        kd_t = at("kd_t", "TOT", [P, 3 * QH, P])
        ss_t = at("ss_t", "DG", [P, 3, QH * DK])
        tot = [f_t]
        off = {1: 0, 2: 4096, 3: 6144, 4: 7168, 5: 7680, 6: 7936, 7: 8064}
        for l in range(1, NLEV + 1):
            tot.append(at(f"tot{l}", "TOT", [P, 2048 >> l], F32, off[l]))
        u_t = at("u_t", "UACC", [P, CT, T + PADW])
        usq = at("usq", "UACC", [P, CT, T])
        acc = at("acc", "UACC", [P, CT, T], F32, 4 * CT * (T + PADW))
        cs_hi = at("cs_hi", "CS", [P, CT, T], F32R)
        cs_lo = at("cs_lo", "CS", [P, CT, T], F32R, 8192)
        xt_t = at("xt_t", "ON0", [P, KT, T])
        xsq = at("xsq", "CS", [P, KT, T])
        ada_c = at("ada_c", "UACC", [P, 8, CHW], F32, 4 * CT * (T + PADW))
        ada_w = [at(f"ada_w{i}", r, [P, KT, CHW]) for i, r in
                 enumerate(("F", "K", "Q", "V", "TOT", "OG", "DG", "ST"))]
        on_hi = [at("on0_hi", "ON0", [P, QH, T], F32R), at("on1_hi", "Q", [P, QH, T], F32R)]
        on_lo = [at("on0_lo", "ON0", [P, QH, T], F32R, 8192), at("on1_lo", "V", [P, QH, T], F32R)]
        mb_t = [at("mb0", "F", [P, 4, T]), at("mb1", "K", [P, 4, T])]
        m_hi = at("m_hi", "CS", [P, KT, T], F32R)
        m_lo = at("m_lo", "TOT", [P, KT, T], F32R)
        ada_acc = at("ada_acc", "UACC", [P, 4, D])
        ada_p = [at("ada_p0", "DG", [P, KT, CHW]), at("ada_p1", "ST", [P, KT, CHW])]
        rows = at("rows", "ON0", [P, 4, D])
        x2_t = at("x2_t", "Q", [P, TT, D])
        h2_t = at("h2_t", "F", [P, TT, D])
        h2T = at("h2T", "TOT", [P, KT, T])
        gffn = at("gffn", "TMP", [P, D])
        cols_t = at("cols_t", "COLS", [P, C_ALL])
        con_t = at("con_t", "CONST", [P, K_ALL])
        mask_t = at("mask_t", "MASK", [P, NLEV * 64], I32)
        tmp = at("tmp", "TMP", [P, 2, T])
        rst = at("rst", "RST", [P, T])
        sc_T = at("sc_T", "RST", [NE, T])
        mod1 = at("mod1", "SMALL", [P, 16])
        cact = at("cact", "SMALL", [P, 8], F32, 64)
        lbc = at("lbc", "SMALL", [P, 32], F32, 96)
        eps_c = at("eps_c", "SMALL", [P, 1], F32, 224)
        nst = at("nst", "SMALL", [P, 8], F32, 256)
        wsel = at("wsel", "SMALL", [P, 2, TT], F32, 288)
        jobs_i = at("jobs_i", "SMALL", [P, NJ + 8], I32, 320)
        nsq = at("nsq", "SMALL", [P, TT, 4], F32, 448)
        idx_s = at("idx_s", "SMALL", [P, NJ], I32, 512)
        idx_g = at("idx_g", "SMALL", [P, NJ], I32, 608)
        gi = at("gi", "SMALL", [P, 1], I32, 704)
        si = at("si", "SMALL", [P, 1], I32, 736)
        rb_t = at("rb_t", "SMALL", [P, NE], F32, 768)
        spacer = [at(f"spacer{i}", "SMALL", [P, 1], F32, 832 + 32 * i) for i in range(2)]
        warm = at("warm", "SMALL", [P, 1], F32, 896)
        e_raw = [at(f"e_raw{c}", r, [P, 2048], F32, o) for c, (r, o) in
                 enumerate((("WRAW", 0), ("WRAW", 8192), ("DG", 0), ("ON0", 0), ("OG", 0), ("ST", 0)))]
        slot_at = (("HT", 0), ("HT", 16384), ("WS", 0), ("WS", 16384), ("UACC", 0), ("CS", 0))
        e_hi = [at(f"e_hi{c}", r, [P, 2048], F32R, o) for c, (r, o) in enumerate(slot_at)]
        e_lo = [at(f"e_lo{c}", r, [P, 2048], F32R, o + 8192) for c, (r, o) in enumerate(slot_at)]
        xg = at("xg", "F", [P, D])
        y_sb = at("y_sb", "F", [P, D], F32, 4096)
        he_hi = at("he_hi", "F", [P, KT * P], F32R, 8192)
        he_lo = at("he_lo", "F", [P, KT * P], F32R, 12288)
        sg_t = at("sg_t", "TOT", [P, FF])
        a_t = at("a_t", "TOT", [P, FF], F32, 2048)
        ae_hi = at("ae_hi", "TOT", [P, 4 * P], F32R, 4096)
        ae_lo = at("ae_lo", "TOT", [P, 4 * P], F32R, 6144)
        gfin = at("gfin", "TMP", [P, D])
        fin = [at("fin0", "HT", [P, 2, D]), at("fin1", "HT", [P, 2, D], F32, 8192),
               at("fin2", "HT", [P, 2, D], F32, 16384), at("fin3", "HT", [P, 2, D], F32, 24576)]
        fsq = at("fsq", "ST", [P, D])
        fsq2 = at("fsq2", "ST", [P, D], F32, 4096)
        rt = at("rt", "ST", [P, 32, TT * NE])

        slot1 = at("slot1", "ST", [P, 2 * TT, P])
        job1 = at("job1", "ST", [P, 2 * TT, NJ], F32, 4 * 28 * TT * NE)

        proj = ctx.enter_context(nc.psum_tensor("proj", [P, 2, 512], F32))
        pp = ctx.enter_context(nc.psum_tensor("pp", [P, 1024], F32))
        ha = ctx.enter_context(nc.psum_tensor("ha", [P, 4, 512], F32))

        ident = con_t[:, K_ID:K_ID + P]
        ones = con_t[:, K_ONE:K_ONE + P]
        mean_d = con_t[:, K_MD:K_MD + P]
        mean_c = con_t[:, K_MC:K_MC + P]
        mean_v = con_t[:, K_MV:K_MV + P]
        tri = con_t[:, K_TRI:K_TRI + P]

        sem = lambda name: ctx.enter_context(nc.semaphore(name))
        s_par = sem("params_loaded")
        s_par2 = sem("masks_loaded")
        s_xt = sem("xT_loaded")
        s_ada = [sem(f"ada_piece{i}_loaded") for i in range(8)]
        s_raw = [sem(f"raw_chunk_loaded{i}") for i in range(2)]
        s_hi = sem("chunk_hi_done")
        s_lo = sem("chunk_lo_done")
        s_tile = sem("tile_done")
        s_free = [sem(f"tile_evacuated{i}") for i in range(2)]
        s_sig = sem("sigmoid_in_tmp")
        s_xsq = sem("xsq_done")
        s_p0 = sem("pre_pe")
        s_eps = sem("eps_set")
        s_cs = sem("c_sigmoid_done")
        s_ca = sem("c_silu_done")
        s_sq0 = sem("x_root_done")
        s_rdone0 = sem("x_root_inverted")
        s_rdone = sem("x_normed")
        s_ac = {pc: sem(f"ada_piece{pc}_accumulated") for pc in ADA_DVE}
        s_md = sem("ada_columns_done")
        s_lb = sem("lower_bounds_done")
        s_h32 = sem("h_float32")
        s_hh = sem("h_hi_done")
        s_hl = sem("h_lo_done")
        s_pad = sem("conv_pad_zeroed")
        s_fd = sem("forget_done")
        s_k = sem("k_done")
        s_dg = sem("dg_done")
        s_lvl = sem("level_done")
        s_st = sem("scores_set")
        s_qu = sem("q_updated")
        s_ku = sem("k_updated")
        s_tot = sem("totals_done")
        s_x1 = sem("kdec_transposed")
        s_kd = sem("kdec_copied")
        s_x2 = sem("state_updates_done")
        s_ss = sem("states_done")
        s_x3 = sem("o_done")
        s_oc = sem("o_copied")
        s_x4 = sem("o_meansq_done")
        s_rt = sem("o_root_done")
        s_or = sem("o_normed")
        s_oo = sem("o_gated")
        s_oh = sem("on_hi_done")
        s_ol = sem("on_lo_done")
        s_cv = sem("conv_steps")
        s_cz = sem("conv_silu_done")
        s_l1 = sem("ln_pe")
        s_ld = sem("ln_dve")
        s_la = sem("ln_act")
        s_ch = sem("cs_hi_done")
        s_cl = sem("cs_lo_done")
        s_mp = sem("merged_sum")
        s_mh = sem("merged_hi_done")
        s_ml = sem("merged_lo_done")
        s_az = sem("ada_acc_zeroed")
        s_ab = sem("ada_bias_loaded")
        s_ap = [sem(f"ada_rest_loaded{i}") for i in range(2)]
        s_aa = sem("ada_accumulated")
        s_ar = sem("ada_rows_pe")
        s_rw = sem("ada_rows_copied")
        s_x = sem("x_loaded")
        s_gf = sem("gffn_loaded")
        s_x2d = sem("x2_done")
        s_xs = sem("x2_act")
        s_n2 = sem("norm2_dve")
        s_xg = sem("x2_times_gain")
        s_nr = sem("x2_sums_reduced")
        s_wm = sem("act_table_warm")
        s_h2 = sem("h2_done")
        s_h2w = sem("h2_written")
        s_h2p = sem("h2_transposed")
        s_h2c = sem("h2T_copied")
        s_lg = sem("logits_done")
        s_sc = sem("router_scores")
        s_r = sem("routing_steps")
        s_dv = sem("choices_done")
        s_rk = sem("ranks_done")
        s_sT = sem("router_scores_transposed")
        s_oh1 = sem("places_one_hot")
        s_ix = sem("index_table_done")
        s_ig = sem("gather_indices_done")
        s_jb = sem("job_table_done")
        s_er = [sem(f"expert_raw{c}_loaded") for c in range(6)]
        s_hg = sem("gate_up_hi_done")
        s_lg2 = sem("gate_up_lo_done")
        s_hd = sem("down_hi_done")
        s_ld2 = sem("down_lo_done")
        s_eu = [sem(f"expert_slot_used{c}") for c in range(6)]
        s_gc = sem("gather_index_copied")
        s_g = sem("tokens_gathered")
        s_xp = sem("tokens_transposed")
        s_heh = sem("tokens_hi_done")
        s_hel = sem("tokens_lo_done")
        s_sg = sem("silu_done")
        s_a = sem("act_done")
        s_ad = sem("act_transposed")
        s_aeh = sem("act_hi_done")
        s_ael = sem("act_lo_done")
        s_y = sem("y_evacuated")
        s_yc = sem("scatter_index_copied")
        s_sp = [sem(f"spacer{i}_set") for i in range(2)]
        s_ys = sem("y_scattered")
        s_fl = [sem(f"final_loaded{i}") for i in range(TT)]
        s_gl = sem("final_gain_loaded")
        s_f1 = sem("final_first_added")
        s_f2 = sem("final_second_added")
        s_fr = sem("final_root_inverted")
        s_fo = sem("final_done")
        s_fa = sem("final_act")
        s_out = sem("out_written")

        block = ctx.enter_context(nc.Block())

        def evacuated(eng, s):
            eng.wait_ge(s_free[s % 2], s // 2 + 1)

        def tile_ready(eng, s):
            eng.wait_ge(s_tile, s + 1)

        last_step = {n: s for s, (_, _, n, _) in enumerate(steps)}

        def chunk_used(eng, n):
            eng.wait_ge(s_tile, last_step[n] + 1)

        def tblk(ap, m, half):
            return ap.rearrange("p (b two m) -> p b two m", two=2, m=m)[:, :, half, :]

        def flat(t):
            return t[:, :, :].rearrange("p h t -> p (h t)") if len(t.shape) == 3 else t[:, :]

        SLOT = {}

        def place(step, what):
            SLOT.setdefault(step, []).append(what)

        for qd in range(2):
            s0 = at_step[("q", 4 * qd + 3)] + 1
            for l in range(NLEV + 1):
                place(s0 + l, ("lev", qd, l))
            for n, x_ in enumerate(("x1", "x2", "x3", "x4")):
                place(s0 + NLEV + 1 + n, (x_, qd))
        place(at_step[("gb", 0)], ("ln", 0))
        place(at_step[("gb", 2)], ("ln", 1))
        O_NORM, O_SPLIT = {}, {}
        for qd in range(2):
            x4_step = at_step[("q", 4 * qd + 3)] + 1 + NLEV + 4
            for h in range(QH):
                O_NORM.setdefault(x4_step + 1 + h, []).append((qd, h))
                O_SPLIT.setdefault(x4_step + 2 + h, []).append((qd, h))
        gn = chunks.index(("ga", 0))
        POOL_SPLITS = [steps[at_step[z]][2] + 1 for z in (("q", 4), ("q", 6), ("gb", 6))]
        POOL_SPLITS += range(gn, len(chunks))
        taps = {(0, 8): 0, (8, 16): 4, (16, 24): 5, (24, 28): 3, (28, 32): 0, (32, 40): 5}
        conv_upto, total_taps = {}, 0
        for (s0, s1), n in taps.items():
            for q in range(s0, s1):
                total_taps += n
                conv_upto[q] = total_taps
        assert total_taps == CW * CT
        merged_steps = [at_step[("ya", i)] for i in range(8)]
        yb0 = at_step[("yb", 0)]
        ADA_AT = [yb0 + 4, yb0 + 6, yb0 + 7] + [q for q in range(at_step[("ga", 0)], at_step[("ya", 7)] + 1) if q % 4 != 3]
        ADA_AT.append(at_step[("ya", 7)])
        assert len(ADA_AT) == 16, len(ADA_AT)
        row_step = at_step[("ya", 7)]
        place(row_step, ("row", 0))
        place(row_step + 2, ("row", 1))

        def chunk_source(n):
            kind, i = chunks[n]
            win = w_in[0].rearrange("(k p) n -> p k n", p=P)
            o = {"q": 0, "fz": 1024, "iv": 2048, "og": 3072, "ca": 4096, "cb": 4608,
                 "ga": 5120, "gb": 6144}
            if kind in o:
                return win[:, :, o[kind] + CHW * i:o[kind] + CHW * (i + 1)]
            if kind == "yb":
                return w_o_conv[0].rearrange("(k p) n -> p k n", p=P)[:, :, 512 * i:512 * (i + 1)]
            w = w_o_hgrn if kind == "ya" else w_out
            return w[0].rearrange("(k p) n -> p k n", p=P)[:, :, CHW * i:CHW * (i + 1)]

        def chunk_view(ap, n):
            return ap[:, n % 2, :].rearrange("p (k n) -> p k n", k=4 if chunks[n][0] == "yb" else 8)

        def expert_view(ap, c):
            return ap[:, :].rearrange("p (k n) -> p k n", k=2 if c >= 4 else 4)

        def expert_load(eng, e, c, part=None):
            w, kk = (w_gate, 4) if c < 2 else (w_up, 4) if c < 4 else (w_down, 2)
            src = w[0].rearrange("e (k p) n -> p e k n", p=P)[:, bass.ds(e, 1), kk * (c % 2):kk * (c % 2) + kk, :]
            dst = e_raw[c][:, :].rearrange("p (o k n) -> p o k n", o=1, k=kk)
            if part:
                dst, src = dst[:, :, 0:1, 0:part], src[:, :, 0:1, 0:part]
            eng.dma_start(dst, src).then_inc(s_er[c], 16)

        NCH = len(chunks)


        @block.sync
        def _(sp):
            sp.dma_start(cols_t[:, :], cols).then_inc(s_par, 16)
            sp.dma_start(con_t[:, :], consts).then_inc(s_par, 16)
            sp.dma_start(xt_t[:, :, :], xT.rearrange("(k p) t -> p k t", p=P)).then_inc(s_xt, 16)
            wa = w_ada[0].rearrange("(k p) n -> p k n", p=P)
            for i in (0, 4, 1, 5, 2, 6, 3, 7):
                sp.dma_start(ada_w[i][:, :, :], wa[:, :, CHW * i:CHW * (i + 1)]).then_inc(s_ada[i], 16)
            for n in range(NCH):
                if n == 2:
                    sp.dma_start(mask_t[:, :], masks).then_inc(s_par2, 16)
                if n >= 2:
                    sp.wait_ge(s_lo, n - 1)
                sp.dma_start(chunk_view(w_raw, n), chunk_source(n)).then_inc(s_raw[n % 2], 16)
                if n == gn - 1:
                    sp.wait_ge(s_az, 1)
                    sp.dma_start(ada_acc[0:1, :, :].rearrange("p a n -> p (a n)"), b_ada_row).then_inc(s_ab, 16)
                if chunks[n] == ("wo", 1):
                    sp.wait_ge(s_ml, KT)
                    sp.dma_start(gffn[:, :], g_ffn.broadcast_to([P, D])).then_inc(s_gf, 16)
                if chunks[n] == ("wo", 0):
                    chunk_used(sp, n - 1)
                    sp.dma_start(x2_t[:, :, :], x.rearrange("(a p) d -> p a d", p=P)).then_inc(s_x, 16)
            sp.wait_ge(s_lo, NCH)
            sp.wait_ge(s_aa, 16 * 8)
            for c in range(3):
                expert_load(sp, 0, c)
            for tt in range(TT):
                sp.wait_ge(s_h2, tt + 1)
                sp.dma_start(h2_dram[P * tt:P * (tt + 1), :], h2_t[:, tt, :]).then_inc(s_h2w, 16)
            expert_load(sp, 0, 3)
            sp.wait_ge(s_n2, 1)
            sp.dma_start(gfin[:, :], g_final.broadcast_to([P, D])).then_inc(s_gl, 16)
            sp.wait_ge(s_lg, 1)
            expert_load(sp, 0, 4)
            sp.wait_ge(s_jb, 1)
            sp.wait_ge(s_ig, 1)
            expert_load(sp, 0, 5)
            sp.wait_ge(s_g, 16)
            e1 = sp.value_load(jobs_i[0:1, 1:2], min_val=0, max_val=NE - 1)
            for c in range(4):
                sp.wait_ge(s_lg2, c + 1)
                expert_load(sp, e1, c)
            before_last = sp.value_load(jobs_i[0:1, NJ:NJ + 1], min_val=14, max_val=21)

            def raw_free(i, c):
                if c < 4:
                    sp.wait_ge(s_lg2, 4 * i + (c - 3))
                else:
                    sp.wait_ge(s_ld2, 2 * i + (c - 7))

            with sp.Fori(2, before_last + 2) as i:
                e = sp.value_load(jobs_i[0:1, bass.ds(i, 1)], min_val=0, max_val=NE - 1)
                ep = sp.value_load(jobs_i[0:1, bass.ds(i - 1, 1)], min_val=0, max_val=NE - 1)
                epp = sp.value_load(jobs_i[0:1, bass.ds(i - 2, 1)], min_val=0, max_val=NE - 1)
                for chunks_, now, before in (((0, 1, 2, 3), e, ep), ((4, 5), ep, epp)):
                    with sp.If(now == before):
                        for c in chunks_:
                            raw_free(i, c)
                            expert_load(sp, now, c, 16)
                    with sp.Else():
                        for c in chunks_:
                            raw_free(i, c)
                            expert_load(sp, now, c)
            for c in (4, 5):
                sp.wait_ge(s_ld2, 2 * before_last + (c - 3))
                expert_load(sp, NE - 1, c)
            sp.wait_ge(s_ys, 16 * before_last + 48)
            for tt in range(TT):
                sp.dma_start(fin[tt][:, :, :], y_dram.rearrange("(c a p) d -> a p c d", c=2, p=P)[tt]).then_inc(s_fl[tt], 16)
            for tt in range(TT):
                sp.wait_ge(s_fo, tt + 1)
                sp.dma_start(out[P * tt:P * (tt + 1), :], fin[tt][:, 0, :]).then_inc(s_out, 16)
            sp.wait_ge(s_out, 16 * TT)

        @block.tensor
        def _(pe):
            def mm3(outap, a_hi, a_lo, b_hi, b_lo, first, last):
                pe.matmul(outap, a_hi, b_hi, start=first, stop=False)
                pe.matmul(outap, a_hi, b_lo, start=False, stop=False)
                return pe.matmul(outap, a_lo, b_hi, start=False, stop=last)

            pe.wait_ge(s_par, 16 * 2)
            for k in range(KT):
                pe.wait_ge(s_xsq, k + 1)
                mm = pe.matmul(pp[:, 0:T], mean_d, xsq[:, k, :], start=(k == 0), stop=(k == KT - 1))
            mm.then_inc(s_p0, 1)
            pe.wait_ge(s_ca, 1)
            for pc in (0, 4, 5, 1, 6, 2, 3, 7):
                if pc not in ADA_DVE:
                    pe.wait_ge(s_ada[pc], 16)
                else:
                    pe.wait_ge(s_ac[pc], KT)
                for j in (2 * pc, 2 * pc + 1):
                    cs = slice(P * (j % 2), P * (j % 2) + P)
                    dst = ha[:, pc % 4, 2 * (pc // 4) + j % 2:2 * (pc // 4) + j % 2 + 1]
                    if pc not in ADA_DVE:
                        for k in range(KT):
                            mm = pe.matmul(dst, ada_w[pc][:, k, cs], cact[:, k:k + 1],
                                           start=(k == 0), stop=(k == KT - 1))
                    else:
                        mm = pe.matmul(dst, ada_c[:, pc, cs], ones[:, 0:1], start=True, stop=True)
                if pc in (4, 1, 2, 7):
                    mm.then_inc(s_p0, 1)

            def level(qd, l):
                if l == 0:
                    for h in range(QH):
                        evacuated(pe, at_step[("q", 4 * qd + h)])
                    pe.wait_ge(s_dg, 4 * qd + 4)
                    if qd == 0:
                        pe.wait_ge(s_sq0, 1)
                    for u in range(NUNIT):
                        mm = pe.matmul(pp[:, u:u + 1], dg_t[:, u // TT, P * (u % TT):P * (u % TT) + P],
                                       ones[:, 0:1], start=True, stop=True)
                    mm.then_inc(s_lvl, 1)
                    return
                m = 1 << (l - 1)
                pe.wait_ge(s_st, 8 * qd + l)
                if l > 1:
                    pe.wait_ge(s_qu, NLEV * qd + l - 1)
                    pe.wait_ge(s_ku, NLEV * qd + l - 1)
                else:
                    pe.wait_ge(s_k, 4 * qd + 4)
                keys = P - m if m >= 16 else P
                for u in range(NUNIT):
                    h, c = u // TT, u % TT
                    mm = pe.matmul(pp[0:keys, 64 * u:64 * u + 64], k_t[:, h, P * c:P * c + keys],
                                   tblk(q_t[:, h, P * c:P * c + P], m, 1), start=True, stop=True)
                mm.then_inc(s_lvl, 1)

            def quad_part(what, qd):
                if what == "x1":
                    pe.wait_ge(s_ku, NLEV * (qd + 1))
                    pe.wait_ge(s_md, 12)
                    if qd:
                        pe.wait_ge(s_rt, 1)
                    for c in range(3):
                        for h in range(QH):
                            mm = pe.transpose(ha[:, c, P * h:P * h + P], k_t[:, h, P * c:P * c + P], ident)
                    mm.then_inc(s_x1, 1)
                elif what == "x2":
                    pe.wait_ge(s_kd, qd + 1)
                    for i in range(4):
                        evacuated(pe, at_step[("iv", 4 * qd + i)])
                    for c in range(3):
                        for h in range(QH):
                            mm = pe.matmul(ha[:, c, P * h:P * h + P], kd_t[:, QH * c + h, :],
                                           v_t[:, c, DK * h:DK * h + DK], start=True, stop=True)
                    mm.then_inc(s_x2, 1)
                elif what == "x3":
                    pe.wait_ge(s_ss, 5 * (qd + 1))
                    pe.wait_ge(s_st, 8 * (qd + 1))
                    pe.wait_ge(s_qu, NLEV * (qd + 1))
                    for h in range(QH):
                        for c in range(TT):
                            o = ha[:, h, P * c:P * c + P]
                            mm = pe.matmul(o, v_t[:, c, DK * h:DK * h + DK], st_t[:, TT * h + c, :],
                                           start=True, stop=(c == 0))
                            if c:
                                mm = pe.matmul(o, ss_t[:, c - 1, DK * h:DK * h + DK],
                                               q_t[:, h, P * c:P * c + P], start=False, stop=True)
                    mm.then_inc(s_x3, 1)
                else:
                    pe.wait_ge(s_oc, 2 * (qd + 1))
                    for h in range(QH):
                        mm = pe.matmul(ha[:, h, :], mean_v, osq[:, h, :], start=True, stop=True)
                    mm.then_inc(s_x4, 1)

            def layernorm_part(n):
                if n == 0:
                    pe.wait_ge(s_cv, CW * CT)
                    pe.wait_ge(s_st, 16)
                else:
                    pe.wait_ge(s_la, 1)
                for ct in range(CT):
                    mm = pe.matmul(pp[:, 512 * n:512 * n + 512], mean_c, (usq if n else acc)[:, ct, :],
                                   start=(ct == 0), stop=(ct == CT - 1))
                mm.then_inc(s_l1, 1)

            def rows_part(n):
                pe.wait_ge(s_aa, 16 * 8)
                if n:
                    pe.wait_ge(s_rw, 1)
                else:
                    pe.wait_ge(s_rt, 2)
                for b in range(4):
                    mm = pe.matmul(ha[:, b, :], ones, ada_acc[:, 2 * n + b // 2, 512 * (b % 2):512 * (b % 2) + 512],
                                   start=True, stop=True)
                mm.then_inc(s_ar, 1)

            for s, (kind, tile, n, t) in enumerate(steps):
                if t == 0:
                    pe.wait_ge(s_lo, n + 1)
                if s >= 2:
                    evacuated(pe, s - 2)
                hi, lo = chunk_view(w_hi, n), chunk_view(w_lo, n)
                bank = proj[:, s % 2, :]
                if kind in ("iv", "wo"):
                    a_hi, a_lo = (h_hi, h_lo) if kind == "iv" else (m_hi, m_lo)
                    for j in range(2):
                        tk = slice(P * (2 * t + j), P * (2 * t + j) + P)
                        for k in range(KT):
                            if kind == "wo" and tile == 0 and j == 0:
                                pe.wait_ge(s_ml, k + 1)
                            mm = mm3(bank[:, CHW * j:CHW * (j + 1)], a_hi[:, k, tk], a_lo[:, k, tk],
                                     hi[:, k, :], lo[:, k, :], k == 0, k == KT - 1)
                else:
                    kk = CT if kind == "yb" else KT
                    for k in range(kk):
                        if s == 0:
                            pe.wait_ge(s_hl, k + 1)
                        if kind == "yb":
                            if tile == 0:
                                pe.wait_ge(s_cl, k + 1)
                            b_hi, b_lo = cs_hi[:, k, :], cs_lo[:, k, :]
                        elif kind == "ya":
                            if tile == 0:
                                pe.wait_ge(s_ol, k + 1)
                            b_hi, b_lo = on_hi[k // QH][:, k % QH, :], on_lo[k // QH][:, k % QH, :]
                        else:
                            b_hi, b_lo = h_hi[:, k, :], h_lo[:, k, :]
                        mm = mm3(bank, hi[:, k, P * t:P * t + P], lo[:, k, P * t:P * t + P],
                                 b_hi, b_lo, k == 0, k == kk - 1)
                mm.then_inc(s_tile, 1)
                for what in SLOT.get(s, ()):
                    if what[0] == "lev":
                        level(what[1], what[2])
                    elif what[0] == "ln":
                        layernorm_part(what[1])
                    elif what[0] == "row":
                        rows_part(what[1])
                    else:
                        quad_part(*what)

            def h2_transpose(tt):
                pe.wait_ge(s_h2, tt + 1)
                if tt == 0:
                    pe.wait_ge(s_rw, 2)
                if tt >= 2:
                    pe.wait_ge(s_h2c, tt - 1)
                for k in range(KT):
                    mm = pe.transpose(ha[:, 2 * (tt % 2) + k // 4, P * (k % 4):P * (k % 4) + P],
                                      h2_t[:, tt, P * k:P * k + P], ident)
                mm.then_inc(s_h2p, 1)

            def logits(tt):
                pe.wait_ge(s_h2c, tt + 1)
                for k in range(KT):
                    mm = pe.matmul(pp[0:NE, P * tt:P * tt + P], cols_t[:, C_WR + NE * k:C_WR + NE * k + NE],
                                   h2T[:, k, P * tt:P * tt + P], start=(k == 0), stop=(k == KT - 1))
                return mm

            h2_transpose(0)
            h2_transpose(1)
            logits(0)
            h2_transpose(2)
            logits(1)
            h2_transpose(3)
            logits(2)
            logits(3).then_inc(s_lg, 1)
            pe.wait_ge(s_sc, 1)
            for tt in range(TT):
                mm = pe.transpose(pp[:, 512 + NE * tt:512 + NE * tt + NE], sc_T[:, P * tt:P * tt + P], ident[0:NE, 0:NE])
            mm.then_inc(s_sT, 1)
            pe.wait_ge(s_dv, 1)
            chosen = rt[:, 20, :]
            pe.matmul(pp[:, 576:640], tri, chosen, start=True, stop=False)
            for t2 in range(TT - 1):
                for tt in range(t2 + 1, TT):
                    pe.matmul(pp[:, 576 + NE * tt:576 + NE * tt + NE], ones, chosen[:, NE * t2:NE * t2 + NE],
                              start=False, stop=(t2 == TT - 2))
            pe.matmul(pp[:, 640:704], ones, chosen, start=True, stop=True).then_inc(s_rk, 1)
            for c in range(2 * TT):
                pe.wait_ge(s_oh1, c + 1)
                mm = pe.matmul(pp[:, 704:704 + NJ], slot1[:, c, :], job1[:, c, :], start=(c == 0), stop=(c == 2 * TT - 1))
            mm.then_inc(s_ix, 1)

            gate_ps, up_ps = proj[:, 0, :], proj[:, 1, :]

            def tokens(i, first=False):
                pe.wait_ge(s_g, 16 * (i + 1))
                if first:
                    pe.wait_ge(s_ig, 1)
                else:
                    pe.wait_ge(s_hel, i)
                for k in range(KT):
                    mm = pe.transpose(pp[:, P * k:P * k + P], xg[:, P * k:P * k + P], ident)
                mm.then_inc(s_xp, 1)

            def half(i, c, ps):
                pe.wait_ge(s_lg2, 4 * i + c + 1)
                hi, lo = expert_view(e_hi[c], c), expert_view(e_lo[c], c)
                for k in range(4):
                    kk = 4 * (c % 2) + k
                    mm = mm3(ps, he_hi[:, P * kk:P * kk + P], he_lo[:, P * kk:P * kk + P],
                             hi[:, k, :], lo[:, k, :], kk == 0, kk == KT - 1)
                mm.then_inc(s_eu[c], 1)

            def gate(i, first=False):
                pe.wait_ge(s_hel, i + 1)
                if not first:
                    pe.wait_ge(s_sg, i)
                half(i, 0, gate_ps)
                half(i, 1, gate_ps)

            def up(i, first=False):
                if not first:
                    pe.wait_ge(s_a, i)
                half(i, 2, up_ps)
                half(i, 3, up_ps)

            def act_t(i, first=False):
                pe.wait_ge(s_a, i + 1)
                if not first:
                    pe.wait_ge(s_ael, i)
                for k in range(4):
                    mm = pe.transpose(ha[:, 0, P * k:P * k + P], a_t[:, P * k:P * k + P], ident)
                mm.then_inc(s_ad, 1)

            def down(i):
                pe.wait_ge(s_ael, i + 1)
                pe.wait_ge(s_y, i + 1)
                for c in (4, 5):
                    pe.wait_ge(s_ld2, 2 * i + c - 3)
                    hi, lo = expert_view(e_hi[c], c), expert_view(e_lo[c], c)
                    for k in range(2):
                        kk = 2 * (c - 4) + k
                        for b in range(2):
                            mm = mm3(ha[:, 1 + b, :], ae_hi[:, P * kk:P * kk + P], ae_lo[:, P * kk:P * kk + P],
                                     hi[:, k, 512 * b:512 * b + 512], lo[:, k, 512 * b:512 * b + 512],
                                     kk == 0, kk == 3)
                    mm.then_inc(s_eu[c], 1)

            tokens(0, True)
            gate(0, True)
            up(0, True)
            tokens(1)
            gate(1)
            act_t(0, True)
            up(1)
            before_last = pe.value_load(jobs_i[0:1, NJ:NJ + 1], min_val=14, max_val=21)
            with pe.Fori(2, before_last + 2) as i:
                tokens(i)
                down(i - 2)
                gate(i)
                act_t(i - 1)
                up(i)
            down(before_last)
            act_t(before_last + 1)
            down(before_last + 1)

        def raw_ready(eng, n):
            eng.wait_ge(s_raw[n % 2], 16 * (n // 2 + 1))

        def expert_raw(eng, j, c):
            eng.wait_ge(s_er[c], 16 * (j + 1))
            return e_raw[c]

        @block.scalar
        def _(act):
            act.wait_ge(s_par, 16 * 2)
            act.activation(cact[:, :], cols_t[:, C_C:C_C + 8], ACT.Sigmoid).then_inc(s_cs, 1)
            act.wait_ge(s_xt, 16)
            for k in range(KT):
                act.activation(xsq[:, k, :], xt_t[:, k, :], ACT.Square).then_inc(s_xsq, 1)
            act.wait_ge(s_eps, 1)
            act.wait_ge(s_p0, 1)
            act.activation(rst[:, :], pp[:, 0:T], ACT.Sqrt, bias=eps_c[:, 0:1]).then_inc(s_sq0, 1)

            def load_table(func, n):
                if n:
                    act.wait_ge(s_wm, n)
                act.activation(warm[:, :], eps_c[:, 0:1], func).then_inc(s_wm, 1)

            def split_hi(n):
                raw_ready(act, n)
                if n >= 2:
                    chunk_used(act, n - 2)
                act.activation(w_hi[:, n % 2, :], w_raw[:, n % 2, :], ACT.Copy).then_inc(s_hi, 1)

            split_hi(0)
            for k in range(KT):
                act.wait_ge(s_md, 3 * (k // 2) + 3)
                act.wait_ge(s_rdone, k // 4 + 1)
                act.activation(h_hi[:, k, :], xt_t[:, k, :], ACT.Identity, scale=mod1[:, 8 + k:9 + k],
                               bias=mod1[:, k:k + 1]).then_inc(s_hh, 1)

            def evacuate(s, kind, tile, n, t):
                bank = proj[:, s % 2, :]
                if kind == "cb":
                    tile_ready(act, s)
                    act.activation(acc[:, tile, :], bank, ACT.Sigmoid).then_inc(s_free[s % 2], 1)
                elif kind == "fz":
                    tile_ready(act, s)
                    if tile >= QH:
                        act.wait_ge(s_qu, 1)
                        act.wait_ge(s_ku, 1)
                        act.wait_ge(s_tot, 1)
                    act.activation(f_t[:, tile % QH, :], bank, ACT.Sigmoid).then_inc(s_free[s % 2], 1)
                elif kind in ("iv", "og"):
                    tile_ready(act, s)
                    before = [q for q in tmp_no if tmp_no[q] == tmp_no[s] - 2]
                    if before:
                        evacuated(act, before[0])
                    act.activation(tmp[:, tmp_no[s] % 2, :], bank, ACT.Sigmoid).then_inc(s_sig, 1)
                elif kind == "gb":
                    tile_ready(act, s)
                    if tile < 4:
                        act.wait_ge(s_qu, NLEV + 1)
                        act.wait_ge(s_ku, NLEV + 1)
                        act.wait_ge(s_tot, NLEV + 1)
                    else:
                        act.wait_ge(s_x1, 2)
                    act.activation(mb_t[tile // 4][:, tile % 4, :], bank, ACT.Sigmoid).then_inc(s_free[s % 2], 1)
                elif kind == "ga":
                    tile_ready(act, s)
                    if tile < 2:
                        evacuated(act, [q for q in tmp_no if tmp_no[q] == tmp_no[s] - 2][0])
                    else:
                        act.wait_ge(s_ml, tile - 1)
                    act.activation(tmp[:, tmp_no[s] % 2, :], bank, ACT.Sigmoid).then_inc(s_free[s % 2], 1)
                elif kind == "ya":
                    act.wait_ge(s_mp, tile + 1)
                    if tile == 0:
                        chunk_used(act, gn - 1)
                    g = at_step[("ga", tile)]
                    act.activation(m_hi[:, tile, :], tmp[:, tmp_no[g] % 2, :], ACT.Copy).then_inc(s_mh, 1)
                elif kind == "wo":
                    if tile == 0:
                        act.wait_ge(s_aa, 16 * 8)
                    act.wait_ge(s_x2d, tile + 1)
                    for j in range(2):
                        tt, q = 2 * t + j, 2 * tile + j
                        if q >= 8:
                            act.wait_ge(s_xs, q - 7)
                        act.activation(fsq[:, CHW * (q % 4):CHW * (q % 4) + CHW] if q % 8 < 4 else
                                       fsq2[:, CHW * (q % 4):CHW * (q % 4) + CHW],
                                       x2_t[:, tt, CHW * (tile // 2):CHW * (tile // 2) + CHW], ACT.Square,
                                       accum_out=nsq[:, tt, tile // 2:tile // 2 + 1]).then_inc(s_xs, 1)

            def o_split(qd, h):
                act.wait_ge(s_oo, QH * qd + h + 1)
                if qd:
                    act.wait_ge(s_x3, 2)
                act.activation(on_hi[qd][:, h, :], o_t[:, h, :], ACT.Copy).then_inc(s_oh, 1)

            def ada_load(g):
                wa = w_ada[0].rearrange("(k p) n -> p k n", p=P)
                if g >= 2:
                    act.wait_ge(s_aa, 8 * (g - 1))
                else:
                    act.wait_ge(s_ol, 2 * QH)
                for pc in range(2):
                    col = 2 * D + CHW * (2 * (g // 2) + pc)
                    kk = slice(4 * (g % 2), 4 * (g % 2) + 4)
                    act.dma_start(ada_p[pc][:, kk, :], wa[:, kk, col:col + CHW]).then_inc(s_ap[g % 2], 16)

            def item(what):
                if what[0] == "x1":
                    act.wait_ge(s_x1, what[1] + 1)
                    act.activation(kd_t[:, :, :].rearrange("p a b -> p (a b)"),
                                   ha[:, 0:3, :].rearrange("p a b -> p (a b)"), ACT.Copy).then_inc(s_kd, 1)
                elif what[0] == "x3":
                    act.wait_ge(s_x3, what[1] + 1)
                    act.activation(o_t[:, :, :], ha[:, :, :], ACT.Copy).then_inc(s_oc, 1)
                    act.activation(osq[:, :, :], ha[:, :, :], ACT.Square).then_inc(s_oc, 1)
                elif what[0] == "x4":
                    act.wait_ge(s_x4, what[1] + 1)
                    act.activation(osq[:, :, :], ha[:, :, :], ACT.Sqrt, bias=eps_c[:, 0:1]).then_inc(s_rt, 1)
                elif what == ("ln", 0):
                    act.wait_ge(s_ld, 1)
                    act.activation(usq[:, :, :], acc[:, :, :], ACT.Square).then_inc(s_la, 1)
                elif what == ("ln", 1):
                    act.wait_ge(s_l1, 2)
                    act.wait_ge(s_rdone, 2)
                    act.activation(rst[:, :], pp[:, 512:1024], ACT.Sqrt, bias=eps_c[:, 0:1]).then_inc(s_la, 1)
                    for ct in range(CT):
                        act.wait_ge(s_ld, 3 + ct)
                        act.activation(usq[:, ct, :], acc[:, ct, :], ACT.Sigmoid,
                                       scale=cols_t[:, C_LG + ct:C_LG + ct + 1],
                                       bias=cols_t[:, C_LB2 + ct:C_LB2 + ct + 1]).then_inc(s_la, 1)
                    for ct in range(CT):
                        act.wait_ge(s_cz, ct + 1)
                        if ct == 0:
                            act.wait_ge(s_p0, 1)
                        act.activation(cs_hi[:, ct, :], acc[:, ct, :], ACT.Copy).then_inc(s_ch, 1)
                elif what[0] == "row":
                    act.wait_ge(s_ar, what[1] + 1)
                    act.activation(rows[:, 2 * what[1]:2 * what[1] + 2, :].rearrange("p a (b n) -> p (a b) n", b=2),
                                   ha[:, :, :], ACT.Copy).then_inc(s_rw, 1)

            for s, (kind, tile, n, t) in enumerate(steps):
                if kind == "wo" and tile == 1:
                    load_table(ACT.Sqrt, 0)
                if t == 0 and n + 1 < NCH:
                    split_hi(n + 1)
                for qd, h in O_SPLIT.get(s, ()):
                    o_split(qd, h)
                evacuate(s, kind, tile, n, t)
                for what in SLOT.get(s, ()):
                    item(what)
                for g in range(16):
                    if s == (ADA_AT[g - 2] if g >= 2 else yb0):
                        ada_load(g)

            act.wait_ge(s_nr, 1)
            act.activation(nst[:, 4:8], nst[:, 0:4], ACT.Sqrt, scale=1.0 / D, bias=eps_c[:, 0:1]).then_inc(s_xs, 1)
            load_table(ACT.Sigmoid, 1)

            def esplit(j, c, first=False):
                src = expert_raw(act, j, c)
                if not first:
                    act.wait_ge(s_eu[c], j)
                act.activation(e_hi[c][:, :], src[:, :], ACT.Copy).then_inc(s_hg if c < 4 else s_hd, 1)

            def h2T_copy(tt):
                act.wait_ge(s_h2p, tt + 1)
                act.activation(h2T[:, :, P * tt:P * tt + P],
                               ha[:, 2 * (tt % 2):2 * (tt % 2) + 2, :].rearrange("p a (k n) -> p (a k) n", n=P),
                               ACT.Copy).then_inc(s_h2c, 1)

            act.wait_ge(s_tile, len(steps))
            esplit(0, 0, True)
            h2T_copy(0)
            h2T_copy(1)
            esplit(0, 1, True)
            h2T_copy(2)
            h2T_copy(3)
            esplit(0, 2, True)
            act.wait_ge(s_lg, 1)
            act.activation(sc_T[:, :], pp[0:NE, 0:T], ACT.Sigmoid).then_inc(s_sc, 1)
            load_table(ACT.Silu, 2)
            esplit(0, 3, True)

            def silu(i, first=False):
                act.wait_ge(s_eu[1], i + 1)
                if not first:
                    act.wait_ge(s_a, i)
                act.activation(sg_t[:, :], gate_ps_(), ACT.Silu).then_inc(s_sg, 1)

            def gate_ps_():
                return proj[:, 0, :]

            def tokens_hi(i, first=False):
                act.wait_ge(s_xp, i + 1)
                if not first:
                    act.wait_ge(s_eu[3], i)
                act.activation(he_hi[:, :], pp[:, :], ACT.Copy).then_inc(s_heh, 1)

            def act_hi(i, first=False):
                act.wait_ge(s_ad, i + 1)
                if not first:
                    act.wait_ge(s_eu[5], i)
                act.activation(ae_hi[:, :], ha[:, 0, :], ACT.Copy).then_inc(s_aeh, 1)

            def body(i, second=False):
                esplit(i, 0)
                esplit(i, 1)
                silu(i - 1, second)
                tokens_hi(i)
                esplit(i, 2)
                esplit(i, 3)
                esplit(i - 1, 4, second)
                esplit(i - 1, 5, second)
                act_hi(i - 1, second)

            tokens_hi(0, True)
            act.wait_ge(s_jb, 1)
            before_last = act.value_load(jobs_i[0:1, NJ:NJ + 1], min_val=14, max_val=21)
            body(1, True)
            with act.Fori(2, before_last + 2) as i:
                body(i)
            silu(before_last + 1)
            for c in (4, 5):
                esplit(before_last + 1, c)
            act_hi(before_last + 1)

            load_table(ACT.Sqrt, 3)

            for tt in range(TT):
                act.wait_ge(s_f2, tt + 1)
                if tt:
                    act.wait_ge(s_fa, 2 * tt - 1)
                act.activation(fsq[:, :], fin[tt][:, 1, :], ACT.Square, accum_out=nst[:, tt:tt + 1]).then_inc(s_fa, 1)
                act.wait_ge(s_fa, 2 * tt + 1)
                act.activation(nst[:, 4 + tt:5 + tt], nst[:, tt:tt + 1], ACT.Sqrt, scale=1.0 / D,
                               bias=eps_c[:, 0:1]).then_inc(s_fa, 1)

        @block.vector
        def _(dve):
            dve.memset(eps_c[:, :], EPS).then_inc(s_eps, 1)
            dve.memset(u_t[:, :, 0:PADW], 0.0).then_inc(s_pad, 1)
            dve.wait_ge(s_par, 16 * 2)
            dve.tensor_tensor(lbc[:, 0:8], cols_t[:, C_LB:C_LB + 8], cols_t[:, C_LB:C_LB + 8],
                              ALU.subtract).then_inc(s_lb, 1)
            dve.wait_ge(s_lb, 1)
            dve.tensor_scalar(lbc[:, 8:16], lbc[:, 0:8], 1.0, None, ALU.add).then_inc(s_lb, 1)
            dve.wait_ge(s_lb, 2)
            dve.tensor_tensor(lbc[:, 0:8], lbc[:, 8:16], lbc[:, 8:16], ALU.subtract).then_inc(s_lb, 1)
            dve.wait_ge(s_lb, 3)
            dve.tensor_scalar(lbc[:, 8:16], lbc[:, 0:8], -1.0, 1.0, ALU.mult, ALU.add).then_inc(s_lb, 1)
            dve.wait_ge(s_cs, 1)
            dve.tensor_tensor(cact[:, :], cact[:, :], cols_t[:, C_C:C_C + 8], ALU.mult).then_inc(s_ca, 1)
            def ada_first(*pieces):
                for k in range(KT):
                    for pc in pieces:
                        if k == 0:
                            dve.wait_ge(s_ada[pc], 16)
                            ins = dve.tensor_scalar(ada_c[:, pc, :], ada_w[pc][:, k, :], cact[:, k:k + 1], None,
                                                    ALU.mult)
                        else:
                            dve.wait_ge(s_ac[pc], k)
                            ins = dve.scalar_tensor_tensor(ada_c[:, pc, :], ada_w[pc][:, k, :], cact[:, k:k + 1],
                                                           ada_c[:, pc, :], ALU.mult, ALU.add)
                        ins.then_inc(s_ac[pc], 1)

            def split_lo(n):
                dve.wait_ge(s_hi, n + 1)
                raw_ready(dve, n)
                if n:
                    dve.wait_ge(s_lo, n)
                dve.tensor_tensor(w_lo[:, n % 2, :], w_raw[:, n % 2, :], w_hi[:, n % 2, :].bitcast(F32),
                                  ALU.subtract).then_inc(s_lo, 1)

            dve.wait_ge(s_ca, 1)
            ada_first(4)
            dve.wait_ge(s_sq0, 1)
            dve.reciprocal(rst[:, :], rst[:, :]).then_inc(s_rdone0, 1)
            def mod_columns(i):
                dve.wait_ge(s_p0, i + 2)
                for n, q in enumerate((2 * i, 8 + 2 * i)):
                    dve.tensor_tensor(mod1[:, q:q + 2], ha[:, i, 2 * n:2 * n + 2], cols_t[:, C_BADA + q:C_BADA + q + 2],
                                      ALU.add).then_inc(s_md, 1)
                dve.wait_ge(s_md, 3 * i + 2)
                dve.scalar_tensor_tensor(mod1[:, 8 + 2 * i:10 + 2 * i], mod1[:, 8 + 2 * i:10 + 2 * i], 1.0,
                                         cols_t[:, C_GMIX + 2 * i:C_GMIX + 2 * i + 2],
                                         ALU.add, ALU.mult).then_inc(s_md, 1)

            def h_low(k):
                dve.wait_ge(s_h32, k + 1)
                dve.wait_ge(s_hh, k + 1)
                dve.tensor_tensor(h_lo[:, k, :], xt_t[:, k, :], h_hi[:, k, :].bitcast(F32),
                                  ALU.subtract).then_inc(s_hl, 1)

            ada_first(1, 2)
            mod_columns(0)
            ada_first(3, 7)
            mod_columns(1)
            mod_columns(2)
            split_lo(0)
            h_low(0)
            h_low(1)
            mod_columns(3)
            for k in range(2, KT):
                h_low(k)

            def evacuate(s, kind, tile, n, t):
                bank = proj[:, s % 2, :]
                free = s_free[s % 2]
                qd, h = tile // QH, tile % QH
                if kind == "ca":
                    evacuated(dve, at_step[("cb", tile)])
                    tile_ready(dve, s)
                    if tile == 0:
                        dve.wait_ge(s_pad, 1)
                    dve.tensor_tensor(u_t[:, tile, PADW:], bank, acc[:, tile, :], ALU.mult).then_inc(free, 1)
                elif kind == "fz":
                    evacuated(dve, s)
                    dve.tensor_scalar(f_t[:, h, :], f_t[:, h, :], lbc[:, 8 + tile:9 + tile],
                                      lbc[:, tile:tile + 1], ALU.mult, ALU.add).then_inc(s_fd, 1)
                elif kind == "q":
                    tile_ready(dve, s)
                    dve.wait_ge(s_k, tile + 1)
                    if qd:
                        dve.wait_ge(s_x3, 1)
                    dve.scalar_tensor_tensor(dg_t[:, h, :], bank, QSCALE, k_t[:, h, :],
                                             ALU.mult, ALU.mult).then_inc(s_dg, 1)
                    dve.scalar_tensor_tensor(q_t[:, h, :], bank, QSCALE, f_t[:, h, :],
                                             ALU.mult, ALU.mult).then_inc(free, 1)
                elif kind == "iv":
                    dve.wait_ge(s_sig, tmp_no2[s] + 1)
                    if qd:
                        dve.wait_ge(s_or, 2 * QH)
                    c0 = CHW * ((tile // 2) % 2)
                    dve.tensor_tensor(v_t[:, 2 * t:2 * t + 2, c0:c0 + CHW],
                                      bank.rearrange("p (a n) -> p a n", a=2),
                                      tmp[:, tmp_no[s] % 2, :].rearrange("p (a n) -> p a n", a=2),
                                      ALU.mult).then_inc(free, 1)
                elif kind == "og":
                    dve.wait_ge(s_sig, tmp_no2[s] + 1)
                    if qd:
                        dve.wait_ge(s_oo, 4)
                    dve.tensor_tensor(og_t[:, h, :], bank, tmp[:, tmp_no[s] % 2, :], ALU.mult).then_inc(free, 1)
                elif kind == "yb":
                    tile_ready(dve, s)
                    evacuated(dve, at_step[("gb", tile)])
                    m = mb_t[tile // 4][:, tile % 4, :]
                    dve.tensor_tensor(m, bank, m, ALU.mult).then_inc(free, 1)
                elif kind == "ya":
                    g = at_step[("ga", tile)]
                    tile_ready(dve, s)
                    evacuated(dve, g)
                    sl = tmp[:, tmp_no[g] % 2, :]
                    dve.tensor_tensor(sl, bank, sl, ALU.mult).then_inc(free, 1)
                    evacuated(dve, s)
                    evacuated(dve, at_step[("yb", tile)])
                    dve.tensor_tensor(sl, sl, mb_t[tile // 4][:, tile % 4, :], ALU.add).then_inc(s_mp, 1)
                    if tile == 7:
                        merged_lo(7)
                elif kind == "wo":
                    tile_ready(dve, s)
                    if tile == 0:
                        dve.wait_ge(s_rw, 1)
                        dve.wait_ge(s_x, 16)
                    else:
                        dve.wait_ge(s_x2d, tile)
                    c0 = CHW * (tile // 2)
                    r2 = rst[:, :].rearrange("p (a n) -> p a n", a=2)
                    dve.tensor_tensor(r2, bank.rearrange("p (a n) -> p a n", a=2),
                                      rows[:, 0:1, c0:c0 + CHW].broadcast_to([P, 2, CHW]), ALU.mult).then_inc(free, 1)
                    evacuated(dve, s)
                    xs = x2_t[:, 2 * t:2 * t + 2, c0:c0 + CHW]
                    dve.tensor_tensor(xs, xs, r2, ALU.add).then_inc(s_x2d, 1)
                    if tile == 3:
                        dve.wait_ge(s_rw, 2)
                        dve.wait_ge(s_gf, 16)
                        dve.scalar_tensor_tensor(rows[:, 2, :], rows[:, 2, :], 1.0, gffn[:, :],
                                                 ALU.add, ALU.mult).then_inc(s_n2, 1)
                        dve.wait_ge(s_n2, 1)
                        dve.wait_ge(s_mp, KT)
                    for old in range(4) if tile == 3 else (tile,) if tile > 3 else ():
                        dve.wait_ge(s_x2d, old + 1)
                        c1 = CHW * (old // 2)
                        ts = slice(2 * (old % 2), 2 * (old % 2) + 2)
                        dve.tensor_tensor(h2_t[:, ts, c1:c1 + CHW], x2_t[:, ts, c1:c1 + CHW],
                                          rows[:, 2:3, c1:c1 + CHW].broadcast_to([P, 2, CHW]),
                                          ALU.mult).then_inc(s_xg, 1)

            conv_at = [0]

            def conv(upto):
                while conv_at[0] < min(upto, CW * CT):
                    i = conv_at[0]
                    w, ct = i // CT, i % CT
                    src = u_t[:, ct, w:w + T]
                    tap = cols_t[:, C_CW + CW * ct + w:C_CW + CW * ct + w + 1]
                    if w == 0:
                        evacuated(dve, at_step[("ca", ct)])
                        dve.tensor_scalar(acc[:, ct, :], src, tap, cols_t[:, C_CB + ct:C_CB + ct + 1],
                                          ALU.mult, ALU.add).then_inc(s_cv, 1)
                    else:
                        dve.wait_ge(s_cv, i - CT + 1)
                        dve.scalar_tensor_tensor(acc[:, ct, :], src, tap, acc[:, ct, :],
                                                 ALU.mult, ALU.add).then_inc(s_cv, 1)
                    conv_at[0] += 1

            def item(what):
                if what[0] == "lev" and what[2] == 0:
                    qd = what[1]
                    dve.wait_ge(s_lvl, 8 * qd + 1)
                    if qd:
                        dve.wait_ge(s_ol, 4)
                    dve.tensor_tensor(st_t[:, :, :], ident.rearrange("p (o n) -> p o n", o=1).broadcast_to([P, NUNIT, P]),
                                      pp[:, 0:NUNIT].rearrange("p (u o) -> p u o", o=1).broadcast_to([P, NUNIT, P]),
                                      ALU.mult).then_inc(s_st, 1)
                elif what[0] == "lev":
                    qd, l = what[1], what[2]
                    m = 1 << (l - 1)
                    dve.wait_ge(s_lvl, 8 * qd + l + 1)
                    dve.wait_ge(s_st, 8 * qd + l)
                    dst = st_t[:, :, :].rearrange("p u (b two m) -> p u b two m", two=2, m=m)[:, :, :, 1, :]
                    if l == 1 and qd == 0:
                        dve.wait_ge(s_par2, 16)
                    msk = mask_t[:, 64 * (l - 1):64 * l].rearrange("p (o b m) -> p o b m", o=1, m=m)
                    dve.copy_predicated(dst, msk.broadcast_to([P, NUNIT, 64 // m, m]),
                                        pp[:, :].rearrange("p (u b m) -> p u b m", u=NUNIT, m=m)).then_inc(s_st, 1)
                    if l == 1:
                        dve.wait_ge(s_fd, 4 * qd + 4)
                    else:
                        dve.wait_ge(s_tot, NLEV * qd + l - 1)
                        dve.wait_ge(s_qu, NLEV * qd + l - 1)
                    qv = tblk(q_t[:, :, :].rearrange("p h t -> p (h t)"), m, 1)
                    tv = flat(tot[l - 1]).rearrange("p (b two) -> p b two", two=2)[:, :, 0:1]
                    dve.tensor_tensor(qv, qv, tv.broadcast_to([P, 1024 // m, m]), ALU.mult).then_inc(s_qu, 1)
                elif what[0] == "x2":
                    qd = what[1]
                    dve.wait_ge(s_x2, qd + 1)
                    dve.tensor_copy(ss_t[:, 0, :], ha[:, 0, :]).then_inc(s_ss, 1)
                    for c in (1, 2):
                        dec = tot[NLEV][:, :].rearrange("p (h c) -> p h c", c=TT)[:, :, c:c + 1]
                        dve.wait_ge(s_ss, 5 * qd + 2 * c - 1)
                        dve.tensor_tensor(ss_t[:, c, :].rearrange("p (h n) -> p h n", h=QH),
                                          ss_t[:, c - 1, :].rearrange("p (h n) -> p h n", h=QH),
                                          dec.broadcast_to([P, QH, DK]), ALU.mult).then_inc(s_ss, 1)
                        dve.wait_ge(s_ss, 5 * qd + 2 * c)
                        dve.tensor_tensor(ss_t[:, c, :], ss_t[:, c, :], ha[:, c, :], ALU.add).then_inc(s_ss, 1)
                elif what == ("ln", 0):
                    dve.wait_ge(s_l1, 1)
                    dve.tensor_tensor(acc[:, :, :], acc[:, :, :],
                                      pp[:, 0:T].rearrange("p (o t) -> p o t", o=1).broadcast_to([P, CT, T]),
                                      ALU.subtract).then_inc(s_ld, 1)
                elif what == ("ln", 1):
                    dve.wait_ge(s_la, 2)
                    dve.reciprocal(rst[:, :], rst[:, :]).then_inc(s_ld, 1)
                    dve.wait_ge(s_ld, 2)
                    for ct in range(CT):
                        dve.tensor_tensor(acc[:, ct, :], acc[:, ct, :], rst[:, :], ALU.mult).then_inc(s_ld, 1)
                    for ct in range(CT):
                        dve.wait_ge(s_la, 3 + ct)
                        dve.tensor_scalar(acc[:, ct, :], acc[:, ct, :], cols_t[:, C_LG + ct:C_LG + ct + 1],
                                          cols_t[:, C_LB2 + ct:C_LB2 + ct + 1], ALU.mult, ALU.add).then_inc(s_ld, 1)
                    for ct in range(CT):
                        dve.wait_ge(s_ld, 7 + ct)
                        dve.tensor_tensor(acc[:, ct, :], acc[:, ct, :], usq[:, ct, :], ALU.mult).then_inc(s_cz, 1)
                    for ct in range(CT):
                        dve.wait_ge(s_ch, ct + 1)
                        dve.tensor_tensor(cs_lo[:, ct, :], acc[:, ct, :], cs_hi[:, ct, :].bitcast(F32),
                                          ALU.subtract).then_inc(s_cl, 1)

            def o_norm(qd, h):
                dve.wait_ge(s_rt, qd + 1)
                dve.reciprocal(osq[:, h, :], osq[:, h, :]).then_inc(s_or, 1)
                dve.wait_ge(s_or, 2 * QH * qd + 2 * h + 1)
                g = cols_t[:, C_ON + 4 * qd + h:C_ON + 4 * qd + h + 1]
                dve.scalar_tensor_tensor(o_t[:, h, :], o_t[:, h, :], g, osq[:, h, :],
                                         ALU.mult, ALU.mult).then_inc(s_or, 1)

            def o_lo(qd, h):
                dve.wait_ge(s_oh, QH * qd + h + 1)
                dve.tensor_tensor(on_lo[qd][:, h, :], o_t[:, h, :], on_hi[qd][:, h, :].bitcast(F32),
                                  ALU.subtract).then_inc(s_ol, 1)

            def ada_half(g):
                for k in range(4):
                    for pc in range(2):
                        col = CHW * (2 * (g // 2) + pc)
                        dst = ada_acc[:, col // D, col % D:col % D + CHW]
                        if k == 0:
                            dve.wait_ge(s_ap[g % 2], 32 * (g // 2 + 1))
                            if g == 0:
                                dve.wait_ge(s_ab, 16)
                        if g % 2 or k:
                            dve.wait_ge(s_aa, 8 * g + 2 * k - 1 + pc)
                        kk = 4 * (g % 2) + k
                        dve.scalar_tensor_tensor(dst, ada_p[pc][:, kk, :], cact[:, kk:kk + 1], dst,
                                                 ALU.mult, ALU.add).then_inc(s_aa, 1)

            def merged_lo(tile):
                dve.wait_ge(s_mh, tile + 1)
                sl = tmp[:, tmp_no[at_step[("ga", tile)]] % 2, :]
                dve.tensor_tensor(m_lo[:, tile, :], sl, m_hi[:, tile, :].bitcast(F32), ALU.subtract).then_inc(s_ml, 1)

            for s, (kind, tile, n, t) in enumerate(steps):
                if t == 0 and n + 1 < NCH and n + 1 not in POOL_SPLITS:
                    split_lo(n + 1)
                for g, at_ in enumerate(ADA_AT):
                    if at_ == s:
                        ada_half(g)
                if s - 1 in merged_steps[:-1]:
                    merged_lo(steps[s - 1][1])
                evacuate(s, kind, tile, n, t)
                for qd, h in O_NORM.get(s, ()):
                    o_norm(qd, h)
                for qd, h in O_SPLIT.get(s, ()):
                    o_lo(qd, h)
                for what in SLOT.get(s, ()):
                    item(what)
                if s in conv_upto:
                    conv(conv_upto[s])

            dve.wait_ge(s_xs, 4 * TT)
            dve.tensor_reduce(nst[:, 0:4], nsq[:, :, :], AX.X, ALU.add).then_inc(s_nr, 1)
            dve.wait_ge(s_xs, 4 * TT + 1)
            dve.reciprocal(nst[:, 4:8], nst[:, 4:8]).then_inc(s_n2, 1)
            dve.wait_ge(s_n2, 2)
            dve.wait_ge(s_xg, 8)
            for tt in range(TT):
                dve.scalar_tensor_tensor(h2_t[:, tt, :], h2_t[:, tt, :], nst[:, 4 + tt:5 + tt], rows[:, 1, :],
                                         ALU.mult, ALU.add).then_inc(s_h2, 1)

            def elo(i, c):
                src = expert_raw(dve, i, c)
                dve.wait_ge(s_hg, 4 * i + c + 1)
                dve.tensor_tensor(e_lo[c][:, :], src[:, :], e_hi[c][:, :].bitcast(F32),
                                  ALU.subtract).then_inc(s_lg2, 1)

            for c in range(3):
                elo(0, c)

            n_r = [0]

            def go(ins):
                n_r[0] += 1
                ins.then_inc(s_r, 1)

            def settle():
                dve.wait_ge(s_r, n_r[0])

            def r(i, a=0, b=TT * NE):
                return rt[:, i, a:b]

            def four(ap):
                return ap.rearrange("p (g e) -> p g e", e=4)

            def col(ap):
                return ap.rearrange("p (g o) -> p g o", o=1)

            def tt_(o, a, b, op):
                go(dve.tensor_tensor(o, a, b, op))

            def by_tt(ap):
                return ap.rearrange("p (a e) -> p a e", a=TT)

            def largest(o, src):
                go(dve.tensor_reduce(o, src, AX.X, ALU.max))

            w4 = con_t[:, K_W4:K_W4 + 4].rearrange("p (o e) -> p o e", o=1)
            dve.wait_ge(s_ys, 16)
            dve.wait_ge(s_sT, 1)
            scores = pp[:, 512:512 + TT * NE]
            tt_(by_tt(r(1)), by_tt(scores), rb_t[:, :].rearrange("p (o e) -> p o e", o=1).broadcast_to([P, TT, NE]), ALU.add)
            go(dve.tensor_copy(r(0), scores))
            settle()
            v = four(r(1))
            pairs = r(1).rearrange("p (g two) -> p g two", two=2)
            mx, mn = r(2, 0, 32), r(2, 32, 64)
            tt_(col(mx), pairs[:, :, 0:1], pairs[:, :, 1:2], ALU.max)
            tt_(col(mn), pairs[:, :, 0:1], pairs[:, :, 1:2], ALU.min)
            settle()
            top_, low, mid, second = [r(3, 16 * a, 16 * a + 16) for a in range(4)]
            halves = lambda ap, i: ap.rearrange("p (g two) -> p g two", two=2)[:, :, i:i + 1]
            tt_(col(top_), halves(mx, 0), halves(mx, 1), ALU.max)
            tt_(col(low), halves(mx, 0), halves(mx, 1), ALU.min)
            tt_(col(mid), halves(mn, 0), halves(mn, 1), ALU.max)
            settle()
            tt_(second, low, mid, ALU.max)
            tt_(four(r(6)), v, col(top_).broadcast_to([P, 16, 4]), ALU.is_equal)
            settle()
            gs, geq, geqw, gone = [r(4, 16 * a, 16 * a + 16) for a in range(4)]
            tt_(gs, top_, second, ALU.add)
            tt_(four(r(7)), four(r(6)), w4.broadcast_to([P, 16, 4]), ALU.mult)
            tt_(four(r(9)), v, col(second).broadcast_to([P, 16, 4]), ALU.is_equal)
            settle()
            largest(r(5, 0, 4), four(gs))
            largest(r(5, 16, 32), four(r(7)))
            settle()
            tt_(four(geq), four(gs), col(r(5, 0, 4)).broadcast_to([P, 4, 4]), ALU.is_equal)
            tt_(four(r(8)), four(r(7)), col(r(5, 16, 32)).broadcast_to([P, 16, 4]), ALU.is_equal)
            settle()
            tt_(four(geqw), four(geq), w4.broadcast_to([P, 4, 4]), ALU.mult)
            tt_(r(10), r(9), r(8), ALU.is_gt)
            settle()
            largest(r(5, 4, 8), four(geqw))
            tt_(four(r(11)), four(r(10)), w4.broadcast_to([P, 16, 4]), ALU.mult)
            settle()
            tt_(four(gone), four(geqw), col(r(5, 4, 8)).broadcast_to([P, 4, 4]), ALU.is_equal)
            largest(r(5, 32, 48), four(r(11)))
            settle()
            tt_(four(r(12)), four(r(11)), col(r(5, 32, 48)).broadcast_to([P, 16, 4]), ALU.is_equal)
            gsel = col(gone).broadcast_to([P, 16, 4])
            tt_(four(r(13)), four(r(8)), gsel, ALU.mult)
            settle()
            tt_(four(r(14)), four(r(12)), gsel, ALU.mult)
            settle()
            dve.tensor_tensor(r(20), r(13), r(14), ALU.add).then_inc(s_dv, 1)
            both = rt[:, 13:15, :].rearrange("p c (a e) -> p (c a) e", e=NE)
            twice = lambda ap: ap.rearrange("p (o n) -> p o n", o=1).broadcast_to([P, 2, TT * NE])
            tt_(rt[:, 15:17, :], twice(r(0)), rt[:, 13:15, :], ALU.mult)
            go(dve.memset(r(19, 0, 16), 0.0))
            settle()
            go(dve.tensor_reduce(wsel[:, :, :].rearrange("p a b -> p (a b)"),
                                 rt[:, 15:17, :].rearrange("p c (a e) -> p (c a) e", e=NE), AX.X, ALU.add))
            settle()
            tt_(r(5, 48, 52), wsel[:, 0, :], wsel[:, 1, :], ALU.add)
            settle()
            go(dve.reciprocal(r(5, 52, 56), r(5, 48, 52)))
            settle()
            tt_(wsel[:, 0, :], wsel[:, 0, :], r(5, 52, 56), ALU.mult)
            tt_(wsel[:, 1, :], wsel[:, 1, :], r(5, 52, 56), ALU.mult)
            dve.wait_ge(s_rk, 1)
            rank, div, slot, job = r(21), r(22), r(23), r(24)
            cnt, nb, incl, start = [r(17, 16 * a, 16 * a + 16) for a in range(4)]
            go(dve.tensor_reduce(cnt, pp[:, 640:704].rearrange("p (a e) -> p e a", a=TT), AX.X, ALU.add))
            go(dve.tensor_copy(rank, pp[:, 576:640]))
            settle()
            go(dve.tensor_scalar(nb, cnt, float(P), 1.0, ALU.is_gt, ALU.add))
            go(dve.tensor_scalar(div, rank, float(P), None, ALU.is_ge))
            settle()
            for b in (2, 3):
                go(dve.scalar_tensor_tensor(nb, cnt, float(P * b), nb, ALU.is_gt, ALU.add))
                go(dve.scalar_tensor_tensor(div, rank, float(P * b), div, ALU.is_ge, ALU.add))
                settle()
            go(dve.tensor_tensor_scan(incl, nb, r(19, 0, 16), 0.0, ALU.add, ALU.add))
            go(dve.scalar_tensor_tensor(slot, div, float(-P), rank, ALU.mult, ALU.add))
            settle()
            tt_(start, incl, nb, ALU.subtract)
            tt_(rt[:, 25:27, :], twice(slot), rt[:, 13:15, :], ALU.mult)
            settle()
            start_b = start.rearrange("p (o e) -> p o e", o=1)
            tt_(by_tt(job), by_tt(div), start_b.broadcast_to([P, TT, NE]), ALU.add)
            go(dve.tensor_reduce(r(18, 0, 8), rt[:, 25:27, :].rearrange("p c (a e) -> p (c a) e", e=NE), AX.X, ALU.add))
            settle()
            tt_(rt[:, 15:17, :], twice(job), rt[:, 13:15, :], ALU.mult)
            settle()
            go(dve.tensor_reduce(r(18, 8, 16), rt[:, 15:17, :].rearrange("p c (a e) -> p (c a) e", e=NE), AX.X, ALU.add))
            settle()
            io = con_t[:, K_IO:K_IO + P]
            tt_(job1[:, :, :], io[:, 0:NJ].rearrange("p (o j) -> p o j", o=1).broadcast_to([P, 2 * TT, NJ]),
                col(r(18, 8, 16)).broadcast_to([P, 2 * TT, NJ]), ALU.is_equal)
            settle()
            tt_(job1[:, :, :], job1[:, :, :], col(con_t[:, K_VAL:K_VAL + 2 * TT]).broadcast_to([P, 2 * TT, NJ]), ALU.mult)
            settle()
            for c in range(2 * TT):
                dve.tensor_scalar(slot1[:, c, :], io, r(18, c, c + 1), None, ALU.is_equal).then_inc(s_oh1, 1)
            ge = rt[:, 21:27, :].rearrange("p a b -> p (a b)").rearrange("p (j e) -> p j e", e=NE)
            tt_(ge, io[:, 0:NJ].rearrange("p (j o) -> p j o", o=1).broadcast_to([P, NJ, NE]),
                start_b.broadcast_to([P, NJ, NE]), ALU.is_ge)
            settle()
            go(dve.tensor_reduce(r(19, 16, 16 + NJ), ge, AX.X, ALU.add))
            settle()
            go(dve.tensor_scalar(jobs_i[:, 0:NJ], r(19, 16, 16 + NJ), -1.0, None, ALU.add))
            settle()
            dve.tensor_scalar(jobs_i[:, NJ:NJ + 1], incl[:, NE - 1:NE], -2.0, None, ALU.add).then_inc(s_jb, 1)
            dve.wait_ge(s_ix, 1)
            go(dve.tensor_scalar(r(27, 0, NJ), pp[:, 704:704 + NJ], 0.0, float(PADIDX + 1), ALU.is_equal, ALU.mult))
            settle()
            go(dve.scalar_tensor_tensor(idx_s[:, :], pp[:, 704:704 + NJ], -1.0, r(27, 0, NJ), ALU.add, ALU.add))
            settle()
            dve.tensor_single_scalar(idx_g[:, :], idx_s[:, :], T - 1, ALU.bitwise_and).then_inc(s_ig, 1)
            dve.memset(nst[:, 0:1], 0.0).then_inc(s_y, 1)
            elo(0, 3)

            def tokens_lo(i):
                dve.wait_ge(s_heh, i + 1)
                dve.tensor_tensor(he_lo[:, :], pp[:, :], he_hi[:, :].bitcast(F32), ALU.subtract).then_inc(s_hel, 1)

            def product(i, first=False):
                dve.wait_ge(s_sg, i + 1)
                dve.wait_ge(s_eu[3], i + 1)
                if not first:
                    dve.wait_ge(s_ad, i)
                dve.tensor_tensor(a_t[:, :], proj[:, 1, :], sg_t[:, :], ALU.mult).then_inc(s_a, 1)

            def act_lo(i):
                dve.wait_ge(s_aeh, i + 1)
                dve.tensor_tensor(ae_lo[:, :], ha[:, 0, :], ae_hi[:, :].bitcast(F32), ALU.subtract).then_inc(s_ael, 1)

            def y_out(i):
                dve.wait_ge(s_eu[5], i + 1)
                dve.wait_ge(s_ys, 16 * (i + 1))
                dve.tensor_tensor(y_sb[:, :], ha[:, 1:3, :].rearrange("p a n -> p (a n)"), rows[:, 3, :],
                                  ALU.mult).then_inc(s_y, 1)

            def body(i, second=False):
                elo(i, 0)
                elo(i, 1)
                product(i - 1, second)
                tokens_lo(i)
                elo(i, 2)
                elo(i, 3)
                if not second:
                    y_out(i - 2)
                act_lo(i - 1)

            tokens_lo(0)
            before_last = dve.value_load(jobs_i[0:1, NJ:NJ + 1], min_val=14, max_val=21)
            body(1, True)
            with dve.Fori(2, before_last + 2) as i:
                body(i)
            product(before_last + 1)
            src = expert_raw(dve, before_last + 1, 4)
            dve.wait_ge(s_hd, 2 * before_last + 3)
            dve.wait_ge(s_ld2, 2 * before_last + 2)
            dve.tensor_tensor(e_lo[4][:, :], src[:, :], e_hi[4][:, :].bitcast(F32), ALU.subtract).then_inc(s_ld2, 1)
            y_out(before_last)
            act_lo(before_last + 1)
            y_out(before_last + 1)

            dve.wait_ge(s_gl, 16)
            for tt in range(TT + 1):
                if tt < TT:
                    dve.wait_ge(s_fl[tt], 16)
                    dve.scalar_tensor_tensor(fin[tt][:, 0, :], fin[tt][:, 0, :], wsel[:, 0, tt:tt + 1], x2_t[:, tt, :],
                                             ALU.mult, ALU.add).then_inc(s_f1, 1)
                    dve.wait_ge(s_f1, tt + 1)
                    dve.scalar_tensor_tensor(fin[tt][:, 1, :], fin[tt][:, 1, :], wsel[:, 1, tt:tt + 1], fin[tt][:, 0, :],
                                             ALU.mult, ALU.add).then_inc(s_f2, 1)
                if tt:
                    q = tt - 1
                    dve.wait_ge(s_fa, 2 * q + 2)
                    dve.reciprocal(nst[:, 4 + q:5 + q], nst[:, 4 + q:5 + q]).then_inc(s_fr, 1)
                    dve.wait_ge(s_fr, q + 1)
                    dve.wait_ge(s_f2, q + 1)
                    dve.scalar_tensor_tensor(fin[q][:, 0, :], fin[q][:, 1, :], nst[:, 4 + q:5 + q], gfin[:, :],
                                             ALU.mult, ALU.mult).then_inc(s_fo, 1)

        @block.gpsimd
        def _(pool):
            pool.dma_start(rb_t[:, :], router_bias.broadcast_to([P, NE])).then_inc(s_ys, 16)
            pool.wait_ge(s_rdone0, 1)
            for half_ in range(2):
                xs = xt_t[:, 4 * half_:4 * half_ + 4, :]
                pool.tensor_tensor(xs, xs, rst[:, :].rearrange("p (o t) -> p o t", o=1).broadcast_to([P, 4, T]),
                                   ALU.mult).then_inc(s_rdone, 1)
            for k in range(KT):
                pool.wait_ge(s_rdone, k // 4 + 1)
                pool.wait_ge(s_md, 3 * (k // 2) + 3)
                pool.wait_ge(s_hh, k + 1)
                pool.tensor_scalar(xt_t[:, k, :], xt_t[:, k, :], mod1[:, 8 + k:9 + k], mod1[:, k:k + 1],
                                   ALU.mult, ALU.add).then_inc(s_h32, 1)

            def totals(qd):
                pool.wait_ge(s_fd, 4 * qd + 4)
                if qd:
                    pool.wait_ge(s_x2, 1)
                    pool.wait_ge(s_ss, 5)
                for l in range(1, NLEV + 1):
                    src = flat(tot[l - 1]).rearrange("p (b two) -> p b two", two=2)
                    if l > 1:
                        pool.wait_ge(s_tot, NLEV * qd + l - 1)
                    pool.tensor_tensor(flat(tot[l]).rearrange("p (b o) -> p b o", o=1), src[:, :, 0:1], src[:, :, 1:2],
                                       ALU.mult).then_inc(s_tot, 1)

            def split_lo(n):
                pool.wait_ge(s_hi, n + 1)
                raw_ready(pool, n)
                pool.wait_ge(s_lo, n)
                pool.tensor_tensor(w_lo[:, n % 2, :], w_raw[:, n % 2, :], w_hi[:, n % 2, :].bitcast(F32),
                                   ALU.subtract).then_inc(s_lo, 1)

            for s, (kind, tile, n, t) in enumerate(steps):
                if t == 0 and n + 1 in POOL_SPLITS:
                    split_lo(n + 1)
                if kind == "fz":
                    pool.wait_ge(s_fd, tile + 1)
                    if tile >= QH:
                        pool.wait_ge(s_x1, 1)
                    pool.tensor_scalar(k_t[:, tile % QH, :], f_t[:, tile % QH, :], -1.0, 1.0,
                                       ALU.mult, ALU.add).then_inc(s_k, 1)
                    if tile % QH == QH - 1:
                        totals(tile // QH)
                for what in SLOT.get(s, ()):
                    if what[0] == "lev" and what[2] > 0:
                        qd, l = what[1], what[2]
                        m = 1 << (l - 1)
                        pool.wait_ge(s_lvl, 8 * qd + l + 1)
                        if l > 1:
                            pool.wait_ge(s_ku, NLEV * qd + l - 1)
                            pool.wait_ge(s_tot, NLEV * qd + l - 1)
                        else:
                            pool.wait_ge(s_k, 4 * qd + 4)
                        kv = tblk(k_t[:, :, :].rearrange("p h t -> p (h t)"), m, 0)
                        tv = flat(tot[l - 1]).rearrange("p (b two) -> p b two", two=2)[:, :, 1:2]
                        pool.tensor_tensor(kv, kv, tv.broadcast_to([P, 1024 // m, m]), ALU.mult).then_inc(s_ku, 1)
                for qd, h in O_NORM.get(s, ()):
                    evacuated(pool, at_step[("og", 4 * qd + h)])
                    pool.wait_ge(s_or, 2 * QH * qd + 2 * h + 2)
                    pool.tensor_tensor(o_t[:, h, :], o_t[:, h, :], og_t[:, h, :], ALU.mult).then_inc(s_oo, 1)
                if (1, QH - 1) in O_NORM.get(s, ()):
                    pool.wait_ge(s_cl, CT)
                    pool.memset(ada_acc[:, :, :], 0.0).then_inc(s_az, 1)

            def gather(i, first=False):
                if not first:
                    pool.wait_ge(s_xp, i)
                    pool.wait_ge(s_g, 16 * i)
                pool.tensor_copy(gi[:, :], idx_g[:, bass.ds(i, 1)]).then_inc(s_gc, 1)
                pool.wait_ge(s_gc, i + 1)
                pool.wait_ge(s_sp[0], i + 1)
                pool.tensor_tensor(spacer[0][:, :], ones[:, 0:1], ones[:, 0:1], ALU.mult).then_inc(s_sp[0], 1)
                pool.indirect_dma_start(xg[:, :], None, h2_dram,
                                        bass.IndirectOffsetOnAxis(ap=gi[:, 0:1], axis=0)).then_inc(s_g, 16)

            def scatter(i):
                pool.wait_ge(s_ys, 16 * (i + 1))
                pool.tensor_copy(si[:, :], idx_s[:, bass.ds(i, 1)]).then_inc(s_yc, 1)
                pool.wait_ge(s_yc, i + 1)
                pool.wait_ge(s_y, i + 2)
                pool.wait_ge(s_sp[1], i + 1)
                pool.tensor_tensor(spacer[1][:, :], ones[:, 0:1], ones[:, 0:1], ALU.mult).then_inc(s_sp[1], 1)
                pool.indirect_dma_start(y_dram, bass.IndirectOffsetOnAxis(ap=si[:, 0:1], axis=0), y_sb[:, :], None,
                                        bounds_check=NPAIR - 1, oob_is_err=False).then_inc(s_ys, 16)

            def down_lo(j, cs=(4, 5)):
                for c in cs:
                    src = expert_raw(pool, j, c)
                    pool.wait_ge(s_hd, 2 * j + c - 3)
                    pool.tensor_tensor(e_lo[c][:, :], src[:, :], e_hi[c][:, :].bitcast(F32),
                                       ALU.subtract).then_inc(s_ld2, 1)

            for sp_ in range(2):
                pool.tensor_tensor(spacer[sp_][:, :], ones[:, 0:1], ones[:, 0:1], ALU.mult).then_inc(s_sp[sp_], 1)
            pool.wait_ge(s_ig, 1)
            pool.wait_ge(s_h2w, 16 * TT)
            pool.wait_ge(s_h2p, TT)
            before_last = pool.value_load(jobs_i[0:1, NJ:NJ + 1], min_val=14, max_val=21)
            gather(0, True)
            gather(1)
            gather(2)
            down_lo(0)
            with pool.Fori(2, before_last + 2) as i:
                gather(i + 1)
                down_lo(i - 1)
                scatter(i - 2)
            pool.wait_ge(s_ld2, 2 * before_last + 3)
            down_lo(before_last + 1, (5,))
            scatter(before_last)
            scatter(before_last + 1)
            pool.wait_ge(s_g, 16 * before_last + 48)


def kernel(**inputs):
    import concourse.bacc as _bacc
    from concourse.bass_utils import run_bass_kernel_spmd as _run

    a = {k: np.ascontiguousarray(v) for k, v in inputs.items()}

    def per_channel(v):
        return v.reshape(-1, P).T

    cols = np.concatenate([
        per_channel(a["c"]), per_channel(a["b_ada"][0, :2 * D]), per_channel(a["norm_mix_g"]),
        per_channel(a["hgrn_lb_logits"][0]), per_channel(a["hgrn_onorm_g"]),
        a["conv_w"][0].T.reshape(CT, P, CW).transpose(1, 0, 2).reshape(P, CT * CW),
        per_channel(a["conv_b"]), per_channel(a["conv_ln_g"]), per_channel(a["conv_ln_b"]),
        a["w_router"].reshape(KT, P, NE).transpose(1, 0, 2).reshape(P, KT * NE)], axis=1)
    one = np.ones((P, P), np.float32)
    consts = np.concatenate([np.eye(P, dtype=np.float32), one, one / D, one / CC, one / DK,
                             np.triu(one, 1), np.tile(np.arange(P, dtype=np.float32), (P, 1)),
                             np.tile(np.array([4, 3, 2, 1], np.float32), (P, 1)),
                             np.array([[c * T + tt * P + p + 1 for c in range(2) for tt in range(TT)]
                                       for p in range(P)], np.float32)], axis=1)
    s = np.arange(P)
    masks = []
    for l in range(NLEV):
        m = 1 << l
        t = np.array([b * 2 * m + m + j for b in range(64 // m) for j in range(m)])
        masks.append((s[:, None] // (2 * m) == t[None, :] // (2 * m)) & (s[:, None] % (2 * m) < m))
    masks = np.concatenate(masks, axis=1).astype(np.int32)

    feed = {
        "xT": a["x"][0].T, "x": a["x"][0], "cols": cols, "consts": consts, "masks": masks,
        "w_ada": a["w_ada"], "b_ada_row": a["b_ada"][:, 2 * D:], "w_in": a["w_in"],
        "w_o_hgrn": a["w_o_hgrn"], "w_o_conv": a["w_o_conv"], "w_out": a["w_out"],
        "router_bias": a["router_bias"].reshape(1, NE), "g_ffn": a["norm_ffn_g"].reshape(1, D),
        "g_final": a["final_norm_g"].reshape(1, D),
        "w_gate": a["w_gate_e"], "w_up": a["w_up_e"], "w_down": a["w_down_e"],
    }
    nc = _bacc.Bacc("TRN2", target_bir_lowering=False, num_devices=1)
    arrays, args = {}, []
    for name, v in feed.items():
        v = np.ascontiguousarray(v)
        arrays[f"in_{name}"] = v
        args.append(nc.dram_tensor(f"in_{name}", v.shape, mybir.dt.from_np(v.dtype), kind="ExternalInput").ap())
    args.append(nc.dram_tensor("h2_rows", (T, D), F32, kind="Internal").ap())
    args.append(nc.dram_tensor("y_rows", (NPAIR, D), F32, kind="Internal").ap())
    args.append(nc.dram_tensor("out_0", (T, D), F32, kind="ExternalOutput").ap())
    trunk_kernel(nc, *args)
    r = _run(nc, [arrays], core_ids=[0])
    return r.results[0]["out_0"].reshape(1, T, D)
```
